# Optimizing a Trainium2 kernel written in Bass

```python
import math
import jax, jax.numpy as jnp
from jax import lax
import numpy as np

D_MODEL = 1024
BATCH = 1
SEQ = 256
DEPTH = 1

N_HEADS = 8
HEAD_DIM = 64
N_KV = 2
GQA = N_HEADS // N_KV
CMP_BLOCK = 32
CMP_STRIDE = 16
SLC_BLOCK = 64
N_SLC = 16
WINDOW = 512
Q_BLOCK = 128
SLC_Q_BLOCK = 64
FORCE_SCORE = 1e4
SCALE = 1.0 / math.sqrt(HEAD_DIM)
CONV_WIDTH = D_MODEL
CONV_K = 3
D_FF = 4 * D_MODEL
EPS = 1e-6
NEG_INF = -1e30

QW = N_HEADS * HEAD_DIM
KVW = N_KV * HEAD_DIM
SPLITS = (QW, KVW, KVW, KVW, KVW, KVW, KVW, 3 * N_HEADS,
          CONV_WIDTH, CONV_WIDTH, CONV_WIDTH, D_MODEL, D_MODEL)
PROJ_WIDTH = sum(SPLITS)
SPLIT_POINTS = tuple(int(v) for v in np.cumsum(SPLITS)[:-1])


def rms_norm(x, g):
    xf = x.astype(jnp.float32)
    y = xf * lax.rsqrt(jnp.mean(xf * xf, axis=-1, keepdims=True) + EPS)
    return (y * g.astype(jnp.float32)).astype(x.dtype)

def alibi_slopes():
    s = 2.0 ** (-8.0 * jnp.arange(1, N_HEADS + 1, dtype=jnp.float32) / N_HEADS)
    return s.reshape(N_KV, GQA)

def masked_softmax(s, mask):
    s = jnp.where(mask, s.astype(jnp.float32), NEG_INF)
    m = jnp.max(s, axis=-1, keepdims=True)
    e = jnp.where(mask, jnp.exp(s - m), 0.0)
    return e / jnp.maximum(jnp.sum(e, axis=-1, keepdims=True), 1e-30)

def compress(k, pos_emb, w):
    B_, S_ = k.shape[0], k.shape[1]
    r = CMP_BLOCK // CMP_STRIDE
    c = k.reshape(B_, S_ // CMP_STRIDE, CMP_STRIDE, N_KV, HEAD_DIM)
    nc = S_ // CMP_STRIDE - r + 1
    blocks = jnp.concatenate([c[:, i:i + nc] for i in range(r)], axis=2)
    blocks = blocks + pos_emb[None, None, :, None, :]
    blocks = blocks.transpose(0, 1, 3, 2, 4).reshape(B_, nc, N_KV, CMP_BLOCK * HEAD_DIM)
    return blocks @ w

def hybrid_layer(x, norm1_g, w_in, q_norm_g, k_norm_g, cmp_pos_k, cmp_pos_v,
                 w_cmp_k, w_cmp_v, conv_w, w_branch_a, w_branch_b, w_out,
                 norm2_g, w_up, w_down):
    B_, S_, _ = x.shape
    xn = rms_norm(x, norm1_g)
    proj = xn @ w_in
    (q, k_c, v_c, k_s, v_s, k_w, v_w, g_nsa, conv_b, conv_c, conv_x,
     gate_a, gate_b) = jnp.split(proj, SPLIT_POINTS, axis=-1)

    q = rms_norm(q.reshape(B_, S_, N_HEADS, HEAD_DIM), q_norm_g)
    q = q.reshape(B_, S_, N_KV, GQA, HEAD_DIM)
    kv_shape = (B_, S_, N_KV, HEAD_DIM)
    k_s = rms_norm(k_s.reshape(kv_shape), k_norm_g[1])
    k_w = rms_norm(k_w.reshape(kv_shape), k_norm_g[2])
    v_s = v_s.reshape(kv_shape)
    v_w = v_w.reshape(kv_shape)
    kc = rms_norm(compress(k_c.reshape(kv_shape), cmp_pos_k, w_cmp_k), k_norm_g[0])
    vc = compress(v_c.reshape(kv_shape), cmp_pos_v, w_cmp_v)

    slopes = alibi_slopes()
    t = jnp.arange(S_)

    nc = kc.shape[1]
    c_start = jnp.arange(nc) * CMP_STRIDE
    c_end = c_start + CMP_BLOCK - 1
    dist_c = (t[:, None] - c_end[None, :]).astype(jnp.float32)
    s_c = (jnp.einsum('bsgrd,bcgd->bgrsc', q, kc).astype(jnp.float32) * SCALE
           - slopes[:, :, None, None] * dist_c)
    p_c = masked_softmax(s_c, dist_c >= 0)
    o_cmp = jnp.einsum('bgrsc,bcgd->bsgrd', p_c.astype(vc.dtype), vc)

    ns = S_ // SLC_BLOCK
    s_start = jnp.arange(ns) * SLC_BLOCK
    overlap = jnp.clip(jnp.minimum(c_start[:, None] + CMP_BLOCK, s_start[None, :] + SLC_BLOCK)
                       - jnp.maximum(c_start[:, None], s_start[None, :]), 0, None)
    overlap = overlap.astype(jnp.float32) / CMP_BLOCK
    imp = jnp.einsum('bgrsc,cj->bgsj', p_c, overlap)
    cur = (t // SLC_BLOCK)[:, None]
    j = jnp.arange(ns)[None, :]
    forced = (j == 0) | (j == cur) | (j == cur - 1)
    score = jnp.where(forced, FORCE_SCORE, jnp.where(j <= cur, imp, -1.0))
    n_sel = min(N_SLC, ns)
    _, sel_idx = lax.top_k(score, n_sel)

    kb = k_s.reshape(B_, ns, SLC_BLOCK, N_KV, HEAD_DIM).transpose(0, 3, 1, 2, 4)
    vb = v_s.reshape(B_, ns, SLC_BLOCK, N_KV, HEAD_DIM).transpose(0, 3, 1, 2, 4)
    gather = jax.vmap(jax.vmap(lambda blk, ids: blk[ids]))
    m_sel = n_sel * SLC_BLOCK

    def sel_chunk(i):
        start = i * SLC_Q_BLOCK
        q_i = lax.dynamic_slice_in_dim(q, start, SLC_Q_BLOCK, axis=1)
        idx_i = lax.dynamic_slice_in_dim(sel_idx, start, SLC_Q_BLOCK, axis=2)
        t_i = start + jnp.arange(SLC_Q_BLOCK)
        ks = gather(kb, idx_i).reshape(B_, N_KV, SLC_Q_BLOCK, m_sel, HEAD_DIM)
        vs = gather(vb, idx_i).reshape(B_, N_KV, SLC_Q_BLOCK, m_sel, HEAD_DIM)
        pos = (idx_i[..., None] * SLC_BLOCK + jnp.arange(SLC_BLOCK)).reshape(B_, N_KV, SLC_Q_BLOCK, m_sel)
        dist = (t_i[None, None, :, None] - pos).astype(jnp.float32)
        s = (jnp.einsum('bqgrd,bgqmd->bgrqm', q_i, ks).astype(jnp.float32) * SCALE
             - slopes[None, :, :, None, None] * dist[:, :, None])
        p = masked_softmax(s, (dist >= 0)[:, :, None])
        return jnp.einsum('bgrqm,bgqmd->bqgrd', p.astype(vs.dtype), vs)

    o_slc = lax.map(sel_chunk, jnp.arange(S_ // SLC_Q_BLOCK))
    o_slc = o_slc.transpose(1, 0, 2, 3, 4, 5).reshape(B_, S_, N_KV, GQA, HEAD_DIM)

    kp = jnp.pad(k_w, ((0, 0), (WINDOW, 0), (0, 0), (0, 0)))
    vp = jnp.pad(v_w, ((0, 0), (WINDOW, 0), (0, 0), (0, 0)))
    span = WINDOW + Q_BLOCK

    def win_chunk(i):
        start = i * Q_BLOCK
        q_i = lax.dynamic_slice_in_dim(q, start, Q_BLOCK, axis=1)
        k_i = lax.dynamic_slice_in_dim(kp, start, span, axis=1)
        v_i = lax.dynamic_slice_in_dim(vp, start, span, axis=1)
        t_i = start + jnp.arange(Q_BLOCK)
        s_pos = start - WINDOW + jnp.arange(span)
        dist = t_i[:, None] - s_pos[None, :]
        mask = (dist >= 0) & (dist < WINDOW) & (s_pos[None, :] >= 0)
        s = (jnp.einsum('bqgrd,bkgd->bgrqk', q_i, k_i).astype(jnp.float32) * SCALE
             - slopes[:, :, None, None] * dist.astype(jnp.float32))
        p = masked_softmax(s, mask)
        return jnp.einsum('bgrqk,bkgd->bqgrd', p.astype(v_i.dtype), v_i)

    o_win = lax.map(win_chunk, jnp.arange(S_ // Q_BLOCK))
    o_win = o_win.transpose(1, 0, 2, 3, 4, 5).reshape(B_, S_, N_KV, GQA, HEAD_DIM)

    g = jax.nn.sigmoid(g_nsa.astype(jnp.float32)).astype(x.dtype).reshape(B_, S_, 3, N_KV, GQA, 1)
    o_nsa = (g[:, :, 0] * o_cmp + g[:, :, 1] * o_slc + g[:, :, 2] * o_win).reshape(B_, S_, QW)

    u = conv_c * conv_x
    y = lax.conv_general_dilated(u, conv_w[:, None, :], window_strides=(1,),
                                 padding=[(CONV_K - 1, 0)],
                                 dimension_numbers=('NWC', 'WIO', 'NWC'),
                                 feature_group_count=CONV_WIDTH)
    z = conv_b * y

    mixed = (jax.nn.sigmoid(gate_a) * (o_nsa @ w_branch_a)
             + jax.nn.sigmoid(gate_b) * (z @ w_branch_b))
    x = x + mixed @ w_out

    h = rms_norm(x, norm2_g)
    return x + jnp.square(jax.nn.relu(h @ w_up)) @ w_down

def first_inputs(seed: int = 0) -> dict:
    key = jax.random.key(seed)
    ks = jax.random.split(key, 16)
    nrm = jax.random.normal
    L = DEPTH
    return {
        "x": nrm(ks[0], (BATCH, SEQ, D_MODEL), jnp.float32),
        "norm1_g": 1.0 + 0.1 * nrm(ks[1], (L, D_MODEL), jnp.float32),
        "w_in": nrm(ks[2], (L, D_MODEL, PROJ_WIDTH), jnp.float32) * D_MODEL ** -0.5,
        "q_norm_g": 1.0 + 0.1 * nrm(ks[3], (L, HEAD_DIM), jnp.float32),
        "k_norm_g": 1.0 + 0.1 * nrm(ks[4], (L, 3, HEAD_DIM), jnp.float32),
        "cmp_pos_k": 0.1 * nrm(ks[5], (L, CMP_BLOCK, HEAD_DIM), jnp.float32),
        "cmp_pos_v": 0.1 * nrm(ks[6], (L, CMP_BLOCK, HEAD_DIM), jnp.float32),
        "w_cmp_k": nrm(ks[7], (L, CMP_BLOCK * HEAD_DIM, HEAD_DIM), jnp.float32) * (CMP_BLOCK * HEAD_DIM) ** -0.5,
        "w_cmp_v": nrm(ks[8], (L, CMP_BLOCK * HEAD_DIM, HEAD_DIM), jnp.float32) * (CMP_BLOCK * HEAD_DIM) ** -0.5,
        "conv_w": nrm(ks[9], (L, CONV_K, CONV_WIDTH), jnp.float32) * CONV_K ** -0.5,
        "w_branch_a": nrm(ks[10], (L, QW, D_MODEL), jnp.float32) * QW ** -0.5,
        "w_branch_b": nrm(ks[11], (L, CONV_WIDTH, D_MODEL), jnp.float32) * CONV_WIDTH ** -0.5,
        "w_out": nrm(ks[12], (L, D_MODEL, D_MODEL), jnp.float32) * D_MODEL ** -0.5,
        "norm2_g": 1.0 + 0.1 * nrm(ks[13], (L, D_MODEL), jnp.float32),
        "w_up": nrm(ks[14], (L, D_MODEL, D_FF), jnp.float32) * D_MODEL ** -0.5,
        "w_down": nrm(ks[15], (L, D_FF, D_MODEL), jnp.float32) * D_FF ** -0.5,
    }

def first_block(x, norm1_g, w_in, q_norm_g, k_norm_g, cmp_pos_k, cmp_pos_v,
              w_cmp_k, w_cmp_v, conv_w, w_branch_a, w_branch_b, w_out,
              norm2_g, w_up, w_down):
    for l in range(DEPTH):
        x = hybrid_layer(x, norm1_g[l], w_in[l], q_norm_g[l], k_norm_g[l],
                         cmp_pos_k[l], cmp_pos_v[l], w_cmp_k[l], w_cmp_v[l],
                         conv_w[l], w_branch_a[l], w_branch_b[l], w_out[l],
                         norm2_g[l], w_up[l], w_down[l])
    return x


N_MEM = 256
CONV_CH = D_MODEL
CONV_WIDTH_2 = 31
HEAD_DIM_2 = D_MODEL // N_HEADS
ATTN_W = N_HEADS * HEAD_DIM_2
IDX_HEADS = 8
IDX_DIM = 64
TOPK_MAX = 256
X_HEADS = 4
X_HEAD_DIM = 128
X_W = X_HEADS * X_HEAD_DIM
D_FF_2 = 4 * D_MODEL

IN_SIZES = (CONV_CH, CONV_CH, ATTN_W, ATTN_W, ATTN_W, IDX_HEADS * IDX_DIM, IDX_DIM, IDX_HEADS, D_MODEL, D_MODEL)
IN_WIDTH = sum(IN_SIZES)


def _rmsnorm(x, g):
    x32 = x.astype(jnp.float32)
    y = x32 * lax.rsqrt(jnp.mean(x32 * x32, axis=-1, keepdims=True) + EPS)
    return y.astype(x.dtype) * g

def _layernorm(x, g, b):
    x32 = x.astype(jnp.float32)
    mu = jnp.mean(x32, axis=-1, keepdims=True)
    xc = x32 - mu
    var = jnp.mean(xc * xc, axis=-1, keepdims=True)
    return (xc * lax.rsqrt(var + EPS)).astype(x.dtype) * g + b

def _split_cols(z, sizes):
    offs = []
    acc = 0
    for s in sizes[:-1]:
        acc += s
        offs.append(acc)
    return jnp.split(z, offs, axis=-1)

def _conformer_conv(a, gate, conv_w, conv_b, ln_g, ln_b, w_out):
    u = a * jax.nn.sigmoid(gate)
    u = lax.conv_general_dilated(
        u, conv_w[:, None, :].astype(u.dtype), window_strides=(1,),
        padding=[(CONV_WIDTH_2 - 1, 0)], dimension_numbers=('NWC', 'WIO', 'NWC'),
        feature_group_count=CONV_CH) + conv_b
    u = jax.nn.silu(_layernorm(u, ln_g, ln_b))
    return u @ w_out

def _dsa_attention(q, k, v, qi, ki, wi):
    B, L = q.shape[0], q.shape[1]
    k_top = min(TOPK_MAX, L // 4)
    nb = L // Q_BLOCK
    key_pos = jnp.arange(L)
    ki32 = ki.astype(jnp.float32)

    def to_blocks(a):
        return a.reshape((B, nb, Q_BLOCK) + a.shape[2:]).swapaxes(0, 1)

    def block(args):
        qb, qib, wb, bi = args
        q_pos = bi * Q_BLOCK + jnp.arange(Q_BLOCK)
        causal = key_pos[None, :] <= q_pos[:, None]
        logits = jnp.einsum('bqhd,bsd->bqhs', qib.astype(jnp.float32), ki32) * (IDX_DIM ** -0.5)
        score = jnp.einsum('bqh,bqhs->bqs', wb.astype(jnp.float32), jax.nn.relu(logits))
        score = jnp.where(causal[None], score, -jnp.inf)
        _, idx = lax.top_k(score, k_top)
        valid = idx <= q_pos[None, :, None]
        k_sel = jax.vmap(lambda kb, ib: kb[ib])(k, idx)
        v_sel = jax.vmap(lambda vb, ib: vb[ib])(v, idx)
        s = jnp.einsum('bqhd,bqkhd->bhqk', qb.astype(jnp.float32), k_sel.astype(jnp.float32)) * (HEAD_DIM_2 ** -0.5)
        s = jnp.where(valid[:, None], s, -jnp.inf)
        p = jax.nn.softmax(s, axis=-1)
        return jnp.einsum('bhqk,bqkhd->bqhd', p.astype(v.dtype), v_sel)

    out = lax.map(block, (to_blocks(q), to_blocks(qi), to_blocks(wi), jnp.arange(nb)))
    return out.swapaxes(0, 1).reshape(B, L, ATTN_W)

def _cross_attention(hn, memn, wq, wkv, wo):
    B, L, _ = hn.shape
    q = (hn @ wq).reshape(B, L, X_HEADS, X_HEAD_DIM)
    kv = memn @ wkv
    k, v = jnp.split(kv, 2, axis=-1)
    k = k.reshape(B, N_MEM, X_HEADS, X_HEAD_DIM)
    v = v.reshape(B, N_MEM, X_HEADS, X_HEAD_DIM)
    s = jnp.einsum('bshd,bmhd->bhsm', q.astype(jnp.float32), k.astype(jnp.float32)) * (X_HEAD_DIM ** -0.5)
    p = jax.nn.softmax(s, axis=-1)
    o = jnp.einsum('bhsm,bmhd->bshd', p.astype(v.dtype), v).reshape(B, L, X_W)
    return o @ wo

def second_inputs(seed: int = 0) -> dict:
    key = jax.random.key(seed)
    ks = jax.random.split(key, 24)
    f32 = jnp.float32

    def w(k, shape, fan_in):
        return jax.random.normal(k, shape, f32) * (fan_in ** -0.5)

    def gain(k, shape):
        return 1.0 + 0.02 * jax.random.normal(k, shape, f32)

    def bias(k, shape):
        return 0.02 * jax.random.normal(k, shape, f32)

    return {
        "x": jax.random.normal(ks[0], (BATCH, SEQ, D_MODEL), f32),
        "mem": jax.random.normal(ks[1], (BATCH, N_MEM, D_MODEL), f32),
        "norm_mix_g": gain(ks[2], (DEPTH, D_MODEL)),
        "w_in": w(ks[3], (DEPTH, D_MODEL, IN_WIDTH), D_MODEL),
        "b_gate": bias(ks[4], (DEPTH, 2 * D_MODEL)),
        "conv_w": w(ks[5], (DEPTH, CONV_WIDTH_2, CONV_CH), CONV_WIDTH_2),
        "conv_b": bias(ks[6], (DEPTH, CONV_CH)),
        "conv_ln_g": gain(ks[7], (DEPTH, CONV_CH)),
        "conv_ln_b": bias(ks[8], (DEPTH, CONV_CH)),
        "w_conv_out": w(ks[9], (DEPTH, CONV_CH, D_MODEL), CONV_CH),
        "w_attn_out": w(ks[10], (DEPTH, ATTN_W, D_MODEL), ATTN_W),
        "w_mix_out": w(ks[11], (DEPTH, D_MODEL, D_MODEL), D_MODEL),
        "norm_x_g": gain(ks[12], (DEPTH, D_MODEL)),
        "norm_mem_g": gain(ks[13], (DEPTH, D_MODEL)),
        "wx_q": w(ks[14], (DEPTH, D_MODEL, X_W), D_MODEL),
        "wx_kv": w(ks[15], (DEPTH, D_MODEL, 2 * X_W), D_MODEL),
        "wx_o": w(ks[16], (DEPTH, X_W, D_MODEL), X_W),
        "norm_ffn_g": gain(ks[17], (DEPTH, D_MODEL)),
        "w_ff1": w(ks[18], (DEPTH, D_MODEL, D_FF_2), D_MODEL),
        "w_ff2": w(ks[19], (DEPTH, D_FF_2, D_MODEL), D_FF_2),
        "norm_final_g": gain(ks[20], (D_MODEL,)),
    }

def second_block(x, mem, norm_mix_g, w_in, b_gate, conv_w, conv_b, conv_ln_g, conv_ln_b,
              w_conv_out, w_attn_out, w_mix_out, norm_x_g, norm_mem_g, wx_q, wx_kv, wx_o,
              norm_ffn_g, w_ff1, w_ff2, norm_final_g):
    B, L, _ = x.shape
    h = x
    for l in range(DEPTH):
        n = _rmsnorm(h, norm_mix_g[l])
        z = n @ w_in[l]
        c_a, c_g, q, k, v, qi, ki, wi, gc_logit, ga_logit = _split_cols(z, IN_SIZES)
        bg_conv, bg_attn = jnp.split(b_gate[l], 2)
        g_conv = jax.nn.sigmoid(gc_logit + bg_conv)
        g_attn = jax.nn.sigmoid(ga_logit + bg_attn)
        y_conv = _conformer_conv(c_a, c_g, conv_w[l], conv_b[l], conv_ln_g[l], conv_ln_b[l], w_conv_out[l])
        qh = q.reshape(B, L, N_HEADS, HEAD_DIM_2)
        kh = k.reshape(B, L, N_HEADS, HEAD_DIM_2)
        vh = v.reshape(B, L, N_HEADS, HEAD_DIM_2)
        qih = qi.reshape(B, L, IDX_HEADS, IDX_DIM)
        wih = wi * (IDX_HEADS ** -0.5)
        y_attn = _dsa_attention(qh, kh, vh, qih, ki, wih) @ w_attn_out[l]
        h = h + (g_conv * y_conv + g_attn * y_attn) @ w_mix_out[l]
        h = h + _cross_attention(_rmsnorm(h, norm_x_g[l]), _rmsnorm(mem, norm_mem_g[l]),
                                 wx_q[l], wx_kv[l], wx_o[l])
        hf = _rmsnorm(h, norm_ffn_g[l]) @ w_ff1[l]
        h = h + jnp.square(jax.nn.relu(hf)) @ w_ff2[l]
    return _rmsnorm(h, norm_final_g)


def setup_inputs(seed=0):
    out = dict(first_inputs(seed))
    for name, value in second_inputs(seed + 1).items():
        if name != "x":
            out[name + "_2"] = value
    return out


def reference(
    x, norm1_g, w_in, q_norm_g, k_norm_g, cmp_pos_k, cmp_pos_v, w_cmp_k, w_cmp_v, conv_w,
    w_branch_a, w_branch_b, w_out, norm2_g, w_up, w_down, mem_2, norm_mix_g_2, w_in_2, b_gate_2,
    conv_w_2, conv_b_2, conv_ln_g_2, conv_ln_b_2, w_conv_out_2, w_attn_out_2, w_mix_out_2,
    norm_x_g_2, norm_mem_g_2, wx_q_2, wx_kv_2, wx_o_2, norm_ffn_g_2, w_ff1_2, w_ff2_2,
    norm_final_g_2,
):
    x = first_block(
        x, norm1_g, w_in, q_norm_g, k_norm_g, cmp_pos_k, cmp_pos_v, w_cmp_k, w_cmp_v, conv_w,
        w_branch_a, w_branch_b, w_out, norm2_g, w_up, w_down,
    )
    return second_block(
        x, mem_2, norm_mix_g_2, w_in_2, b_gate_2, conv_w_2, conv_b_2, conv_ln_g_2, conv_ln_b_2,
        w_conv_out_2, w_attn_out_2, w_mix_out_2, norm_x_g_2, norm_mem_g_2, wx_q_2, wx_kv_2,
        wx_o_2, norm_ffn_g_2, w_ff1_2, w_ff2_2, norm_final_g_2,
    )


_drawn_inputs = setup_inputs


def setup_inputs(seed=0):
    import zlib

    import numpy as np

    out = dict(_drawn_inputs(seed))
    spreads = {}
    factors = {'q_norm_g': 3.203,
     'k_norm_g': 3.974,
     'cmp_pos_k': 8.0,
     'norm_mix_g_2': 5.628,
     'b_gate_2': 8.0,
     'conv_b_2': 6.58,
     'conv_ln_g_2': 8.0,
     'conv_ln_b_2': 8.0,
     'norm_x_g_2': 8.0,
     'norm_mem_g_2': 8.0,
     'norm_ffn_g_2': 11.317,
     'norm_final_g_2': 8.061}
    for name, (base, spread) in spreads.items():
        noise = np.random.default_rng([zlib.crc32(name.encode()), seed]).standard_normal(out[name].shape)
        drawn = base * np.exp(spread * noise) if base else spread * noise
        out[name] = __import__('jax').numpy.asarray(drawn.astype(out[name].dtype))
    for name, factor in factors.items():
        out[name] = (out[name] * factor).astype(out[name].dtype)
    return out
```

```python
from contextlib import ExitStack

from functools import partial

import numpy as np

import concourse.bass as bass
from concourse import mybir

F32 = mybir.dt.float32
F32R = mybir.dt.float32r
ALU = mybir.AluOpType
ACT = mybir.ActivationFunctionType
AX = mybir.AxisListType

P = 128
D = 1024
UC = 2048
NRAW = 3
NW = 3
EPS = 1e-6
NEG = -1e30

PRM = {}
_n = 0
for _name, _w in (("norm1", 8), ("norm2", 8), ("convw", 24), ("normmix", 8), ("convw2", 248), ("convb2", 8),
                  ("lng", 8), ("lnb", 8), ("normx", 8), ("normmem", 8), ("normffn", 8), ("qg", 1), ("kg", 3),
                  ("posk", 32), ("posv", 32)):
    PRM[_name] = _n
    _n += _w
NPRM = _n
CS = {"ident": 0, "ones": 128, "dist": 256, "causal": 640, "end": 1024}
C2 = {"cbias": 0, "cmask": 480, "end": 960}


def signalling(fn, sem, n):
    fn().then_inc(sem, n)


class Engine:

    def __init__(self, eng, sem):
        self.eng, self.sem, self.count, self.seen, self.queue = eng, sem, 0, {}, []

    def wait(self, *tokens):
        for t in tokens:
            if t is None:
                continue
            if isinstance(t, list):
                self.wait(*t)
                continue
            sem, val = t
            if self.seen.get(sem.name, 0) < val:
                self.seen[sem.name] = val
                self.queue.append(partial(self.eng.wait_ge, sem, val))

    def __call__(self, fn, *tokens, done=True):
        self.wait(*tokens)
        if not done:
            self.queue.append(fn)
            return None
        self.count += 1
        self.queue.append(partial(signalling, fn, self.sem, 1))
        return (self.sem, self.count)

    def last(self):
        return (self.sem, self.count) if self.count else None


def build(nc, A, out):
    ctx = ExitStack()
    with ctx:
        def sb(name, cols, dt=F32):
            return ctx.enter_context(nc.sbuf_tensor(name, [P, cols], dt))

        def sem(name):
            return ctx.enter_context(nc.semaphore(name))

        raw = [sb(f"raw{i}", UC) for i in range(NRAW)]
        whi = [sb(f"whi{i}", UC, F32R) for i in range(NW)]
        wlo = [sb(f"wlo{i}", UC, F32R) for i in range(NW)]
        XT = sb("XT", 8 * 512, F32R)
        ZT = sb("ZT", 8 * 512, F32R)
        OT = sb("OT", 8 * 512, F32R)
        X = sb("X", 2 * D)
        CST = sb("CST", CS["end"])
        PR = sb("PR", NPRM)
        KV = sb("KV", 2048)
        ST = sb("ST", 512)
        W = sb("W", 16240)
        PB = [ctx.enter_context(nc.psum_tensor(f"pb{i}", [P, 512], F32)) for i in range(8)]

        pe = Engine(nc.tensor, sem("done_pe"))
        act = Engine(nc.scalar, sem("done_act"))
        dve = Engine(nc.vector, sem("done_dve"))
        pool = Engine(nc.gpsimd, sem("done_pool"))
        sp = Engine(nc.sync, sem("done_sp"))
        s_raw = [sem(f"raw_landed{i}") for i in range(NRAW)]
        n_raw = [0] * NRAW
        sems = [0]

        def dma(dst, src, *tokens):
            s = sem(f"load{sems[0]}")
            sems[0] += 1
            sp.wait(*tokens)
            sp.queue.append(partial(signalling, partial(nc.sync.dma_start, dst, src), s, 16))
            return (s, 16)

        def fence():
            return [e.last() for e in (pe, act, dve, pool)]

        ident = CST[:, 0:128]
        ones = CST[:, 128:256]
        distb = CST[:, 256:640]
        causal = CST[:, 640:1024]

        def prm(name, i=0, n=1, rows=P):
            return PR[0:rows, PRM[name] + i:PRM[name] + i + n]

        st_at = [0]

        def stat(n):
            if st_at[0] + n > 496:
                st_at[0] = 0
            a = st_at[0]
            st_at[0] += n
            return ST[:, a:a + n]

        keep_at = [960]

        def keep(n):
            keep_at[0] += n
            assert keep_at[0] <= 2048
            return KV[:, keep_at[0] - n:keep_at[0]]

        free = {"main": [(b, None) for b in range(4)], "aux": [(b, None) for b in range(4, 8)]}

        def take(kind):
            return free[kind].pop(0)

        def give(kind, bank, *tokens):
            free[kind].append((bank, list(tokens)))

        units = []
        landed, split_hi, split_lo, used = {}, {}, {}, {}

        def unit_rows(w, kt0, nk, n0, n):
            units.append((w[kt0 * P:(kt0 + nk) * P, n0:n0 + n].rearrange("(k p) n -> p k n", p=P), nk, n))
            return len(units) - 1

        def load(u):
            if u >= len(units):
                return
            src, nk, n = units[u]
            i = u % NRAW
            if u >= NRAW:
                sp.wait(split_lo[u - NRAW])
            parts = src if isinstance(src, list) else [(src, 0, n)]
            view = raw[i][:, 0:nk * n].rearrange("p (k n) -> p k n", k=nk)
            for s, c0, w in parts:
                n_raw[i] += 16
                sp.queue.append(partial(signalling, partial(nc.sync.dma_start, view[:, :, c0:c0 + w], s), s_raw[i], 16))
            landed[u] = (s_raw[i], n_raw[i])

        split_at = [0]

        def split(u):
            _, nk, n = units[u]
            c = nk * n
            r, h, l = raw[u % NRAW][:, 0:c], whi[u % NW][:, 0:c], wlo[u % NW][:, 0:c]
            split_hi[u] = act(partial(nc.scalar.activation, h, r, ACT.Copy), landed[u], used.get(u - NW))
            split_lo[u] = dve(partial(nc.vector.tensor_tensor, l, r, h.bitcast(F32), ALU.subtract), split_hi[u])
            load(u + NRAW)

        side = []

        def pump(n=1):
            for _ in range(n):
                for g in list(side):
                    if next(g, StopIteration) is StopIteration:
                        side.remove(g)

        def flush():
            k = 0
            while side:
                pump()
                k += 1
                assert k < 1000

        def use(u, fn, pumps=1):
            assert u == len(used)
            while split_at[0] < min(u + NW, len(units)):
                split(split_at[0])
                split_at[0] += 1
            _, nk, n = units[u]
            h = whi[u % NW][:, 0:nk * n].rearrange("p (k n) -> p k n", k=nk)
            l = wlo[u % NW][:, 0:nk * n].rearrange("p (k n) -> p k n", k=nk)
            used[u] = fn(h, l, [split_hi[u], split_lo[u]])
            pump(pumps)

        def mm(o, l, r, start, stop, *tokens, done=False):
            return pe(partial(nc.tensor.matmul, o, l, r, start=start, stop=stop, skip_group_check=True), *tokens, done=done)

        def rows_group(us, T, toks, n, finish, kt_at=0, pumps=1):
            banks = [take("main") for _ in range(2)]
            nks = sum(units[u][1] for u in us)
            kt = 0
            for u in us:
                def fn(h, l, tokens):
                    nonlocal kt
                    for k in range(units[u][1]):
                        for t in range(2):
                            o = PB[banks[t][0]][:, 0:n]
                            xh = T[:, (kt_at + kt) * 512 + t * P:(kt_at + kt) * 512 + t * P + P]
                            xl = T[:, (kt_at + kt) * 512 + 256 + t * P:(kt_at + kt) * 512 + 256 + t * P + P]
                            mm(o, xh, h[:, k, :], kt == 0, False, tokens, toks[kt_at + kt], banks[t][1])
                            mm(o, xh, l[:, k, :], False, False)
                            last = mm(o, xl, h[:, k, :], False, kt == nks - 1,
                                      done=(k == units[u][1] - 1 and t == 1) or kt == nks - 1)
                            if kt == nks - 1:
                                got[t] = last
                        kt += 1
                    return last
                got = {}
                use(u, fn, pumps)
            for t in range(2):
                rel = finish(t, PB[banks[t][0]][:, 0:n], got[t])
                give("main", banks[t][0], rel)

        def cols_group(us, T, toks, finish, pumps=1, nf=4):
            banks = [take("main") for _ in range(nf)]
            kt = 0
            got = {}
            for i, u in enumerate(us):
                def fn(h, l, tokens):
                    nk = units[u][1]
                    for f in range(nf):
                        o = PB[banks[f][0]]
                        for k in range(nk):
                            a = (kt + k) * 512
                            mm(o[:, :], h[:, k, f * P:f * P + P], T[:, a:a + 512], kt + k == 0, False,
                               tokens, toks[kt + k], banks[f][1])
                            fin = i == len(us) - 1 and k == nk - 1
                            last = mm(o[:, 0:256], l[:, k, f * P:f * P + P], T[:, a:a + 256], False, fin,
                                      done=fin or (k == nk - 1 and f == nf - 1))
                        if i == len(us) - 1:
                            got[f] = last
                            rel = finish(f, o[:, 0:256], o[:, 256:512], last)
                            give("main", banks[f][0], rel)
                    return last
                use(u, fn, pumps)
                kt += units[u][1]

        rt_at = [0]
        RT = W[:, 15216:15728].rearrange("p (i n) -> p i n", i=2)
        rt_free = [None, None]

        def join(dst, L, R, tok, *tokens):
            i = rt_at[0] % 2
            rt_at[0] += 1
            a = act(partial(nc.scalar.activation, RT[:, i, :], R, ACT.Copy), tok, rt_free[i])
            d = dve(partial(nc.vector.tensor_tensor, dst, L, RT[:, i, :], ALU.add), a, *tokens)
            rt_free[i] = d
            return d

        def halves(dst, src, *tokens):
            h = act(partial(nc.scalar.activation, dst[:, 0:256], src, ACT.Copy), *tokens)
            return dve(partial(nc.vector.tensor_tensor, dst[:, 256:512], src, dst[:, 0:256].bitcast(F32), ALU.subtract), h)

        def rsqrt(dst, src, scale, *tokens):
            n = src.shape[1]
            rows = src.shape[0]
            a, b = stat(n)[0:rows, :], stat(n)[0:rows, :]
            t = dve(partial(nc.vector.tensor_scalar, a, src, scale, EPS, ALU.mult, ALU.add), *tokens)
            t2 = act(partial(nc.scalar.activation, b, a, ACT.Sqrt), t)
            return dve(partial(nc.vector.reciprocal, dst, b), t2)

        def to_T(src, toks, dst, gain, *tokens):
            out_tok = {}
            for j in range(4):
                while not free["aux"]:
                    yield
                bank, rel = take("aux")
                for k in range(2):
                    for t in range(2):
                        s = src[:, t * D + (2 * j + k) * P:t * D + (2 * j + k) * P + P]
                        o = PB[bank][:, k * 256 + t * P:k * 256 + t * P + P]
                        tt = pe(partial(nc.tensor.transpose, o, s, ident), toks[t], rel, const_tok,
                                done=(k == 1 and t == 1))
                if gain is None:
                    b = PB[bank][:, :].rearrange("p (k n) -> p k n", k=2)
                    d = dst[:, 2 * j * 512:(2 * j + 2) * 512].rearrange("p (k h n) -> p k h n", k=2, h=2)
                    h = act(partial(nc.scalar.activation, d[:, :, 0, :], b, ACT.Copy), tt, *tokens)
                    l = dve(partial(nc.vector.tensor_tensor, d[:, :, 1, :], b, d[:, :, 0, :].bitcast(F32),
                                                                ALU.subtract), h, *tokens)
                    out_tok[2 * j] = out_tok[2 * j + 1] = [h, l]
                else:
                    hs = []
                    for k in range(2):
                        kt = 2 * j + k
                        b = PB[bank][:, k * 256:k * 256 + 256]
                        g = prm(gain, kt)
                        h = act(partial(nc.scalar.activation, dst[:, kt * 512:kt * 512 + 256], b, ACT.Copy,
                                                                       scale=g), tt, *tokens)
                        hs.append(h)
                    for k in range(2):
                        kt = 2 * j + k
                        b = PB[bank][:, k * 256:k * 256 + 256]
                        g = prm(gain, kt)
                        l = dve(partial(nc.vector.scalar_tensor_tensor, 
                            out=dst[:, kt * 512 + 256:kt * 512 + 512], in0=b, scalar=g,
                            in1=dst[:, kt * 512:kt * 512 + 256].bitcast(F32), op0=ALU.mult, op1=ALU.subtract),
                            hs[1], *tokens)
                        out_tok[kt] = [hs[k], l]
                give("aux", bank, out_tok[2 * j], out_tok[2 * j + 1])
                yield out_tok
            yield out_tok

        def drain(g):
            last = None
            for v in g:
                if v is not None:
                    last = v
            return last

        def norm_rows(src, dst, sq, src_toks, *tokens):
            out_t = []
            for t in range(2):
                ss, r = stat(1), stat(1)
                s = src[:, t * D:t * D + D]
                a = act(partial(nc.scalar.activation, sq[:, 0:D], s, ACT.Square, accum_out=ss),
                        src_toks[t], *tokens, *out_t[-1:])
                q = rsqrt(r, ss, 1.0 / D, a)
                d = dst[:, t * D:t * D + D]
                out_t.append(dve(partial(nc.vector.tensor_scalar, d, s, r, None, ALU.mult), q, *tokens))
            return out_t

        w_in, w_in2 = A["w_in"], A["w_in_2"]
        G = {}

        def rows_units(name, w, n0, n, kts=8, kt0=0):
            G[name] = [unit_rows(w, kt0 + k, 4, n0, n) for k in range(0, kts, 4)]

        rows_units("b1_q", w_in, 0, 512)
        rows_units("b1_kv", w_in, 512, 512)
        rows_units("b1_w", w_in, 1024, 280)
        for i in range(2):
            for nm, o in (("c", 2328), ("x", 3352), ("b", 1304)):
                rows_units(f"b1_{nm}{i}", w_in, o + 512 * i, 512)
        for nm, o in (("ga", 4376), ("gb", 5400)):
            for i in range(2):
                rows_units(f"b1_{nm}{i}", w_in, o + 512 * i, 512)
        for i in range(2):
            rows_units(f"b1_wa{i}", A["w_branch_a"], 512 * i, 512, 4)
        for i in range(2):
            rows_units(f"b1_wb{i}", A["w_branch_b"], 512 * i, 512)
        for i in range(2):
            rows_units(f"b1_wo{i}", A["w_out"], 512 * i, 512)

        def ffn_units(tag, up, down):
            def dn(c):
                for i in range(2):
                    rows_units(f"{tag}_dn{c}_{i}", down, 512 * i, 512, 4, 4 * c)
            for c in range(8):
                rows_units(f"{tag}_up{c}", up, 512 * c, 512)
                if c:
                    dn(c - 1)
            dn(7)

        ffn_units("f1", A["w_up"], A["w_down"])
        rows_units("mk", A["wx_kv_2"], 0, 512)
        rows_units("mv", A["wx_kv_2"], 512, 512)
        rows_units("b2_qi", w_in2, 5120, 512)
        ki = w_in2[:, 5632:5696].rearrange("(k p) n -> p k n", p=P)
        wi = w_in2[:, 5696:5704].rearrange("(k p) n -> p k n", p=P)
        units.append(([(ki, 0, 64), (ki, 64, 64), (wi, 128, 8)], 8, 136))
        G["b2_ki"] = [len(units) - 1]
        for i in range(2):
            rows_units(f"b2_cg{i}", w_in2, 1024 + 512 * i, 512)
            rows_units(f"b2_ca{i}", w_in2, 512 * i, 512)
        for nm, o in (("k", 3072), ("q", 2048)):
            for i in range(2):
                rows_units(f"b2_{nm}{i}", w_in2, o + 512 * i, 512)
        for i in range(2):
            rows_units(f"b2_v{i}", w_in2, 4096 + 512 * i, 512)
        for nm, o in (("ga", 6728), ("gc", 5704)):
            for i in range(2):
                rows_units(f"b2_{nm}{i}", w_in2, o + 512 * i, 512)
        for i in range(2):
            rows_units(f"b2_wa{i}", A["w_attn_out_2"], 512 * i, 512)
        for i in range(2):
            rows_units(f"b2_wc{i}", A["w_conv_out_2"], 512 * i, 512)
        for i in range(2):
            rows_units(f"b2_wm{i}", A["w_mix_out_2"], 512 * i, 512)
        rows_units("xq", A["wx_q_2"], 0, 512)
        for i in range(2):
            rows_units(f"xo{i}", A["wx_o_2"], 512 * i, 512, 4)
        ffn_units("f2", A["w_ff1_2"], A["w_ff2_2"])

        xv = A["x"].rearrange("o (t p) d -> p (o t) d", p=P)
        x_tok = [dma(X[:, 0:D], xv[:, 0, :]), dma(X[:, D:2 * D], xv[:, 1, :])]
        const_tok = dma(CST[:, :], A["consts"])
        prm_tok = dma(PR[:, :], A["params"])
        for u in range(NRAW):
            load(u)
        c2_tok = dma(KV[:, 0:960], A["consts2"])
        cbias = KV[:, 0:480].rearrange("p (t n) -> p t n", t=2)
        cmask = KV[:, 480:960].rearrange("p (t n) -> p t n", t=2)

        QKV = W[:, 0:2608].rearrange("p (t n) -> p t n", t=2)
        TT = W[:, 2608:6704].rearrange("p (h n) -> p h n", h=16)
        WC = W[0:64, 6704:8752].rearrange("p (j e) -> p j e", j=32)
        PTC = W[0:30, 6704:8752].rearrange("p (h n) -> p h n", h=8)
        KP = W[0:64, 8752:9712].rearrange("p (b j) -> p b j", j=32)
        SP_ = W[:, 10480:11632].rearrange("p (i n) -> p i n", i=3)
        PT = W[:, 11632:12784].rearrange("p (i n) -> p i n", i=3)
        CC = W[:, 12784:13808].rearrange("p (f n) -> p f n", f=4)
        UU = W[:, 13808:14840].rearrange("p (f n) -> p f n", f=4)
        Y1 = W[:, 9712:9968]
        Y2 = W[:, 9968:10224]
        PC = W[:, 8752:9232].rearrange("p (t n) -> p t n", t=2)
        SQ = W[:, 2608:3632]

        wc_tok = dma(WC, A["wcmp"][:, 0:2048].rearrange("p (j e) -> p j e", j=32))

        SX = W[:, 4096:6144]
        n1 = norm_rows(X, SX, SQ, x_tok)
        xt = drain(to_T(SX, n1, XT, "norm1", prm_tok))
        early = fence()

        qkv_tok = []

        def copy_out(c0, n):
            def fin(t, bank, tok):
                r = act(partial(nc.scalar.activation, QKV[:, t, c0:c0 + n], bank, ACT.Copy), tok)
                qkv_tok.append(r)
                return r
            return fin

        rows_group(G["b1_q"], XT, xt, 512, copy_out(0, 512))
        rows_group(G["b1_kv"], XT, xt, 512, copy_out(512, 512))
        rows_group(G["b1_w"], XT, xt, 280, copy_out(1024, 280))

        ring_at = [0]
        sp_free, pt_free = [None] * 3, [None] * 3

        def head_scores(qT, kT, *tokens):
            bank, rel = take("aux")
            mm(PB[bank][:, 0:128], qT[:, 0:128], kT[:, 0:128], True, False, rel, *tokens)
            return bank, mm(PB[bank][:, 128:384], qT[:, 128:256], kT[:, 0:256], False, True, done=True)

        def head_softmax(bank, tok, bias, pre, post, gate, *tokens):
            i = ring_at[0] % 3
            ring_at[0] += 1
            s = SP_[:, i, :]
            a = dve(partial(nc.vector.scalar_tensor_tensor, out=s, in0=PB[bank][:, 0:384], scalar=pre, in1=bias,
                                                     op0=ALU.mult, op1=ALU.add), tok, sp_free[i], *tokens)
            give("aux", bank, a)
            m, nm, sm, ri, gi = stat(2), stat(2), stat(2), stat(2), stat(2)
            dve(partial(nc.vector.tensor_reduce, m[:, 0:1], s[:, 0:128], AX.X, ALU.max), a)
            b = dve(partial(nc.vector.tensor_reduce, m[:, 1:2], s[:, 128:384], AX.X, ALU.max), a)
            c = dve(partial(nc.vector.tensor_scalar, nm, m, -post, None, ALU.mult), b)
            act(partial(nc.scalar.activation, s[:, 0:128], s[:, 0:128], ACT.Exp, bias=nm[:, 0:1], scale=post,
                                       accum_out=sm[:, 0:1]), c)
            d = act(partial(nc.scalar.activation, s[:, 128:384], s[:, 128:384], ACT.Exp, bias=nm[:, 1:2], scale=post,
                                           accum_out=sm[:, 1:2]), c)
            yield
            f = dve(partial(nc.vector.reciprocal, ri, sm), d)
            if gate is not None:
                f = dve(partial(nc.vector.tensor_tensor, gi, ri, gate, ALU.mult), f)
                ri = gi
            dve(partial(nc.vector.tensor_scalar, s[:, 0:128], s[:, 0:128], ri[:, 0:1], None, ALU.mult), f)
            g = dve(partial(nc.vector.tensor_scalar, s[:, 128:384], s[:, 128:384], ri[:, 1:2], None, ALU.mult), f)
            yield i, g

        def head_PT(i, tok):
            s = SP_[:, i, :]
            bank, rel = take("aux")
            o = PB[bank]
            for j in range(3):
                t = pe(partial(nc.tensor.transpose, o[:, j * P:j * P + P], s[:, j * P:j * P + P], ident), tok, rel,
                       done=(j == 2))
            sp_free[i] = t
            c = act(partial(nc.scalar.activation, PT[:, i, :], o[:, 0:384], ACT.Copy), t, pt_free[i])
            give("aux", bank, c)
            return c

        def bank_halves(p, b, *tokens):
            hh = act(partial(nc.scalar.activation, OT[:, p * 512:p * 512 + 256], PB[b][:, 0:256], ACT.Copy), *tokens)
            ll = dve(partial(nc.vector.tensor_tensor, OT[:, p * 512 + 256:p * 512 + 512], PB[b][:, 0:256],
                                               OT[:, p * 512:p * 512 + 256].bitcast(F32), ALU.subtract), hh)
            give("aux", b, ll)
            return [hh, ll]

        def in_flight(n, start, finished):
            active, nxt = [], 0
            while nxt < n or active:
                for it in list(active):
                    if next(it[1], StopIteration) is StopIteration:
                        active.remove(it)
                        finished(it[0])
                if nxt < n and len(active) < 3 and len(free["aux"]) >= 2:
                    it = start(nxt)
                    next(it)
                    active.append((nxt, it))
                    nxt += 1
                yield

        def b1_side():
            sq = SQ
            SS, RS, GG, GE = keep(24), keep(24), keep(48), keep(48)
            ssv = SS.rearrange("p (t h) -> p t h", t=2)
            rsv = RS.rearrange("p (t h) -> p t h", t=2)
            parts = ((0, 8, 0), (768, 2, 8), (1024, 2, 10))
            for c0, nh, h0 in parts:
                s = QKV[:, :, c0:c0 + 64 * nh]
                q = sq[:, 0:128 * nh]
                a = act(partial(nc.scalar.activation, q.rearrange("p (t n) -> p t n", t=2), s, ACT.Square),
                        qkv_tok, early, dve.last())
                r = dve(partial(nc.vector.tensor_reduce, 
                    ssv[:, :, h0:h0 + nh], q.rearrange("p (t h d) -> p t h d", t=2, d=64), AX.X, ALU.add), a)
            rr = rsqrt(RS, SS, 1.0 / 64, r)
            ge = act(partial(nc.scalar.activation, GE.rearrange("p (t n) -> p t n", t=2), QKV[:, :, 1280:1304], ACT.Exp,
                                            scale=-1.0), qkv_tok)
            g1 = dve(partial(nc.vector.tensor_scalar, GE, GE, 1.0, None, ALU.add), ge)
            g_tok = dve(partial(nc.vector.reciprocal, GG, GE), g1)
            ggv = GG.rearrange("p (t b h) -> p t b h", t=2, b=3)
            yield
            nt = []
            for c0, nh, h0 in parts:
                for t in range(2):
                    s = QKV[:, t, c0:c0 + 64 * nh].rearrange("p (h d) -> p h d", d=64)
                    r = rsv[:, t, h0:h0 + nh].unsqueeze(2).broadcast_to([P, nh, 64])
                    nt.append(dve(partial(nc.vector.tensor_tensor, s, s, r, ALU.mult), rr))
            yield
            tt_tok = {}
            jobs = [(12, 512, None), (14, 640, None)] + [(2 * i, 128 * i, ("qg", 0)) for i in range(4)] + \
                   [(8, 768, ("kg", 1)), (10, 1024, ("kg", 2))]
            for n, (h0, c0, gain) in enumerate(jobs):
                while not free["aux"]:
                    yield
                bank, rel = take("aux")
                for j in range(2):
                    for t in range(2):
                        o = PB[bank][0:64, j * 256 + t * P:j * 256 + t * P + P]
                        s = QKV[:, t, c0 + 64 * j:c0 + 64 * j + 64]
                        tk = pe(partial(nc.tensor.transpose, o, s, ident), nt[-1], qkv_tok, rel,
                                done=(j == 1 and t == 1))
                d = TT[0:64, h0:h0 + 2, :].rearrange("p h n -> p (h n)")
                b = PB[bank][0:64, :]
                if gain is None:
                    c = act(partial(nc.scalar.activation, d, b, ACT.Copy), tk)
                else:
                    g = prm(gain[0], gain[1], 1, 64)
                    c = act(partial(nc.scalar.activation, d, b, ACT.Copy, scale=g), tk)
                give("aux", bank, c)
                tt_tok[h0] = tt_tok[h0 + 1] = c
                if n % 2:
                    yield
            while not free["aux"]:
                yield
            bank, rel = take("aux")
            kpf = None
            wtok = wc_tok
            for which, (h0, pos) in enumerate(((12, "posk"), (14, "posv"))):
                for g in range(2):
                    for half in range(2):
                        s = TT[0:64, h0 + g, 16 * half:16 * half + 240].rearrange("p (c j) -> p c j", j=16)
                        d = KP[:, 15 * g:15 * g + 15, 16 * half:16 * half + 16]
                        pp = prm(pos, 16 * half, 16, 64).unsqueeze(1).broadcast_to([64, 15, 16])
                        kt = dve(partial(nc.vector.tensor_tensor, d, s, pp, ALU.add), tt_tok[h0], kpf)
                yield
                for j in range(32):
                    kpf = mm(PB[bank][0:30, 64 * which:64 * which + 64], KP[:, :, j], WC[:, j, :], j == 0, j == 31,
                             kt, wtok, rel, done=(j == 31))
                if which == 0:
                    wtok = dma(WC, A["wcmp"][:, 2048:4096].rearrange("p (j e) -> p j e", j=32), kpf)
                yield
            kc = keep(128)[0:30, :]
            c = act(partial(nc.scalar.activation, kc, PB[bank][0:30, 0:128], ACT.Copy), kpf)
            give("aux", bank, c)
            ks2, kss, krs = keep(64)[0:30, :], stat(1)[0:30, :], stat(1)[0:30, :]
            a = act(partial(nc.scalar.activation, ks2, kc[:, 0:64], ACT.Square, accum_out=kss), c)
            r = rsqrt(krs, kss, 1.0 / 64, a)
            kn = dve(partial(nc.vector.tensor_scalar, ks2, kc[:, 0:64], krs, None, ALU.mult), r)
            yield
            bank, rel = take("aux")
            t = pe(partial(nc.tensor.transpose, PB[bank][0:64, 0:30], ks2, ident[0:30, 0:30]), kn, rel)
            kcn = keep(30)[0:64, :]
            kcn_t = act(partial(nc.scalar.activation, kcn, PB[bank][0:64, 0:30], ACT.Copy, scale=prm("kg", 0, 1, 64)), t)
            give("aux", bank, kcn_t)
            yield
            pcs = []
            for t in range(2):
                bank, rel = take("aux")
                for h in range(8):
                    m = mm(PB[bank][:, 30 * h:30 * h + 30], TT[0:64, h, t * P:t * P + P], kcn, h == 0, h == 7,
                           rel, kcn_t, tt_tok[h], done=(h == 7))
                pc = PC[:, t, :]
                pcv = pc.rearrange("p (h n) -> p h n", h=8)
                mx, sm, ri, gi = stat(8), stat(8), stat(8), stat(8)
                a = dve(partial(nc.vector.scalar_tensor_tensor, 
                    out=pc, in0=PB[bank][:, 0:240], scalar=0.125, in1=cbias[:, t, :], op0=ALU.mult, op1=ALU.add),
                    m, c2_tok)
                give("aux", bank, a)
                b = dve(partial(nc.vector.tensor_reduce, mx, pcv, AX.X, ALU.max), a)
                c = dve(partial(nc.vector.tensor_tensor, pcv, pcv, mx.unsqueeze(2).broadcast_to([P, 8, 30]),
                                                                  ALU.subtract), b)
                x = act(partial(nc.scalar.activation, pc, pc, ACT.Exp), c)
                f = dve(partial(nc.vector.tensor_tensor, pc, pc, cmask[:, t, :], ALU.mult), x)
                f = dve(partial(nc.vector.tensor_reduce, sm, pcv, AX.X, ALU.add), f)
                f = dve(partial(nc.vector.tensor_scalar, sm, sm, 1e-30, None, ALU.max), f)
                f = dve(partial(nc.vector.reciprocal, ri, sm), f)
                f = dve(partial(nc.vector.tensor_tensor, gi, ri, ggv[:, t, 0, :], ALU.mult), f, g_tok)
                pcs.append(dve(partial(nc.vector.tensor_tensor, 
                    pcv, pcv, gi.unsqueeze(2).broadcast_to([P, 8, 30]), ALU.mult), f))
                yield
            ptc = {}
            for p in range(4):
                while not free["aux"]:
                    yield
                bank, rel = take("aux")
                for j in range(2):
                    for t in range(2):
                        o = PB[bank][0:30, j * 256 + t * P:j * 256 + t * P + P]
                        s = PC[:, t, 30 * (2 * p + j):30 * (2 * p + j) + 30]
                        tk = pe(partial(nc.tensor.transpose, o, s, ident), pcs[1], rel, done=(j == 1 and t == 1))
                ptc[p] = act(partial(nc.scalar.activation, 
                    PTC[:, 2 * p:2 * p + 2, :].rearrange("p h n -> p (h n)"), PB[bank][0:30, :], ACT.Copy), tk, kpf)
                give("aux", bank, ptc[p])
            yield

            def item(h, branch, acc):
                g = h // 4
                koff = (8, 10)[branch]
                voff = (896, 1152)[branch]
                while not free["aux"]:
                    yield
                bank, tk = head_scores(TT[0:64, h, :], TT[0:64, koff + g, :], tt_tok[h], tt_tok[koff])
                slope = 2.0 ** -(h + 1)
                for v in head_softmax(bank, tk, distb, 0.125 / slope, slope, ggv[:, :, 1 + branch, h], g_tok):
                    if v is None:
                        yield
                i, tk = v
                yield
                while not free["aux"]:
                    yield
                c = head_PT(i, tk)
                yield
                o = PB[acc[0]]
                r0 = 64 * (h % 2)
                if branch == 0:
                    mm(o[r0:r0 + 64, 0:256], kc[:, 64:128], PTC[:, h, :], True, False, acc[1], ptc[h // 2])
                mm(o[r0:r0 + 64, 0:256], QKV[:, 0, voff + 64 * g:voff + 64 * g + 64], PT[:, i, 0:256], False, False, c)
                pt_free[i] = mm(o[r0:r0 + 64, 128:256], QKV[:, 1, voff + 64 * g:voff + 64 * g + 64],
                                PT[:, i, 256:384], False, branch == 1, done=True)
                done_items[h] = pt_free[i]

            done_items = {}
            accs = {}
            n_done = {}

            def start(j):
                h, b = j // 2, j % 2
                if h // 2 not in accs:
                    accs[h // 2] = take("aux")
                return item(h, b, accs[h // 2])

            def finished(j):
                p = j // 4
                n_done[p] = n_done.get(p, 0) + 1
                if n_done[p] == 4:
                    b = accs[p][0]
                    o_tok[p] = bank_halves(p, b, done_items[2 * p], done_items[2 * p + 1])

            yield from in_flight(16, start, finished)

        o_tok = {}
        side.append(b1_side())

        z_tok = {}
        u0 = dve(partial(nc.vector.memset, UU[:, :, 0:2], 0.0))
        cc_tok, uu_free, uu_tok = {}, [None] * 4, {}
        y_free = [None]

        def fin_c(i):
            def fin(f, L, R, tok):
                cc_tok[f] = join(CC[:, f, :], L, R, tok)
                return cc_tok[f]
            return fin

        def fin_x(i):
            def fin(f, L, R, tok):
                d = join(UU[:, f, 2:258], L, R, tok, u0)
                uu_tok[f] = dve(partial(nc.vector.tensor_tensor, UU[:, f, 2:258], UU[:, f, 2:258], CC[:, f, :], ALU.mult),
                                d, cc_tok[f])
                return d
            return fin

        def fin_b(i):
            def fin(f, L, R, tok):
                ft = 4 * i + f
                u = UU[:, f, :]
                d = dve(partial(nc.vector.tensor_scalar, Y1, u[:, 0:256], prm("convw", ft), None, ALU.mult),
                        uu_tok[f], y_free[0])
                for k in (1, 2):
                    d = dve(partial(nc.vector.scalar_tensor_tensor, out=Y1, in0=u[:, k:k + 256],
                                                                  scalar=prm("convw", 8 * k + ft), in1=Y1,
                                                                  op0=ALU.mult, op1=ALU.add), d)
                j = join(Y2, L, R, tok, y_free[0])
                z = dve(partial(nc.vector.tensor_tensor, Y2, Y2, Y1, ALU.mult), j)
                z_tok[ft] = y_free[0] = halves(ZT[:, ft * 512:ft * 512 + 512], Y2, z)
                return j
            return fin

        for i in range(2):
            cols_group(G[f"b1_c{i}"], XT, xt, fin_c(i))
            cols_group(G[f"b1_x{i}"], XT, xt, fin_x(i))
            cols_group(G[f"b1_b{i}"], XT, xt, fin_b(i))
        flush()
        after_attn = fence()

        GA = W[:, 0:2048].rearrange("p (t n) -> p t n", t=2)
        GB = W[:, 2048:4096].rearrange("p (t n) -> p t n", t=2)
        MX = W[:, 4096:6144]
        MXv = MX.rearrange("p (t n) -> p t n", t=2)
        TMP = W[:, 6144:8192].rearrange("p (i n) -> p i n", i=4)
        g_toks = {}

        def fin_gate(G_, i, key):
            def fin(t, bank, tok):
                r = act(partial(nc.scalar.activation, G_[:, t, 512 * i:512 * i + 512], bank, ACT.Sigmoid), tok, after_attn)
                g_toks[key, i, t] = r
                return r
            return fin

        for i in range(2):
            rows_group(G[f"b1_ga{i}"], XT, xt, 512, fin_gate(GA, i, "a"))
        for i in range(2):
            rows_group(G[f"b1_gb{i}"], XT, xt, 512, fin_gate(GB, i, "b"))

        mx_tok = {}

        def fin_first(i, G_, key):
            def fin(t, bank, tok):
                r = dve(partial(nc.vector.tensor_tensor, MXv[:, t, 512 * i:512 * i + 512], bank,
                                                  G_[:, t, 512 * i:512 * i + 512], ALU.mult),
                        tok, g_toks[key, i, t], after_attn)
                mx_tok[i, t] = r
                return r
            return fin

        def fin_second(i, G_, key):
            def fin(t, bank, tok):
                x = TMP[:, 2 * i + t, :]
                r = dve(partial(nc.vector.tensor_tensor, x, bank, G_[:, t, 512 * i:512 * i + 512], ALU.mult),
                        tok, g_toks[key, i, t], after_attn)
                m = MXv[:, t, 512 * i:512 * i + 512]
                mx_tok[i, t] = dve(partial(nc.vector.tensor_tensor, m, m, x, ALU.add), r, mx_tok[i, t])
                return r
            return fin

        for i in range(2):
            rows_group(G[f"b1_wa{i}"], OT, o_tok, 512, fin_first(i, GA, "a"))
        for i in range(2):
            rows_group(G[f"b1_wb{i}"], ZT, z_tok, 512, fin_second(i, GB, "b"))
        xn_free = pe.last()
        mt = drain(to_T(MX, [[mx_tok[0, t], mx_tok[1, t]] for t in range(2)], XT, None, xn_free))

        x_cur = {}

        def fin_add(i, *tokens):
            def fin(t, bank, tok):
                m = X[:, t * D + 512 * i:t * D + 512 * i + 512]
                r = dve(partial(nc.vector.tensor_tensor, m, m, bank, ALU.add), tok, *tokens)
                x_cur[i, t] = r
                return r
            return fin

        def x_toks():
            return [[x_cur[0, t], x_cur[1, t]] for t in range(2)]

        for i in range(2):
            rows_group(G[f"b1_wo{i}"], XT, mt, 512, fin_add(i))

        SQB = W[:, 8192:9216]
        HF = W[:, 9216:9728].rearrange("p (i n) -> p i n", i=2)
        XS = W[:, 4096:6144]
        hf_free = [None, None]

        def ffn(tag, xt_toks):
            assert len(free["aux"]) == 4
            accs = [take("aux") for _ in range(4)]
            ht_free = [None, None]
            ht = {}
            k_n = [0]

            def up(c):
                def fin(f, L, R, tok):
                    i = (4 * c + f) % 2
                    j = join(HF[:, i, :], L, R, tok, hf_free[i])
                    v = dve(partial(nc.vector.scalar_tensor_tensor, out=HF[:, i, :], in0=HF[:, i, :], scalar=0.0,
                                                             in1=HF[:, i, :], op0=ALU.max, op1=ALU.mult), j)
                    a = (4 * (c % 2) + f) * 512
                    h = act(partial(nc.scalar.activation, ZT[:, a:a + 256], HF[:, i, :], ACT.Copy), v, ht_free[c % 2])
                    l = dve(partial(nc.vector.tensor_tensor, ZT[:, a + 256:a + 512], HF[:, i, :],
                                                      ZT[:, a:a + 256].bitcast(F32), ALU.subtract), h)
                    hf_free[i] = l
                    ht[c, f] = [h, l]
                    return j
                cols_group(G[f"{tag}_up{c}"], XT, xt_toks, fin)

            def down(c):
                for i in range(2):
                    u = G[f"{tag}_dn{c}_{i}"][0]

                    def fn(h, l, tokens):
                        for k in range(4):
                            for t in range(2):
                                b, rel = accs[2 * i + t]
                                o = PB[b][:, :]
                                a = (4 * (c % 2) + k) * 512
                                xh, xl = ZT[:, a + t * P:a + t * P + P], ZT[:, a + 256 + t * P:a + 256 + t * P + P]
                                mm(o, xh, h[:, k, :], c == 0 and k == 0, False, tokens, ht[c, k], rel)
                                mm(o, xh, l[:, k, :], False, False)
                                last = mm(o, xl, h[:, k, :], False, c == 7 and k == 3, done=(k == 3))
                                if k == 3:
                                    fin_tok[i, t] = last
                        return last
                    use(u, fn)
                ht_free[c % 2] = pe.last()

            fin_tok = {}
            for c in range(8):
                up(c)
                if c:
                    down(c - 1)
            down(7)
            for i in range(2):
                for t in range(2):
                    b, _ = accs[2 * i + t]
                    r = fin_add(i)(t, PB[b][:, :], fin_tok[i, t])
                    give("aux", b, r)

        def norm_to_XT(gain, sq_free=None):
            w_free = pe.last()
            n = norm_rows(X, XS, SQB, x_toks(), w_free)
            return to_T(XS, n, XT, gain, w_free)

        MEM = W[:, 0:2048]
        MS = W[:, 2048:4096]
        ht = drain(norm_to_XT("norm2"))
        f0 = fence()
        memv = A["mem_2"].rearrange("o (t p) d -> p (o t) d", p=P)
        mem_tok = [dma(MEM[:, 0:D], memv[:, 0, :], f0), dma(MEM[:, D:2 * D], memv[:, 1, :], f0)]
        mn = norm_rows(MEM, MS, SQB, mem_tok, f0)
        memT = drain(to_T(MS, mn, OT, "normmem", f0))
        ffn("f1", ht)

        KXT = KV[:, 0:1024].rearrange("p (h n) -> p h n", h=4)
        VX = KV[:, 1024:2048].rearrange("p (t n) -> p t n", t=2)
        b2x = norm_to_XT("normmix")
        kx_tok, vx_tok = {}, {}
        xt = {}

        def b2x_side():
            for v in b2x:
                if v is not None:
                    xt.update(v)
                yield

        def fin_kx(f, L, R, tok):
            kx_tok[f] = join(KXT[:, f, :], L, R, tok)
            return kx_tok[f]

        def fin_vx(t, bank, tok):
            vx_tok[t] = act(partial(nc.scalar.activation, VX[:, t, :], bank, ACT.Copy), tok)
            return vx_tok[t]

        cols_group(G["mk"], OT, memT, fin_kx)
        side.append(b2x_side())
        rows_group(G["mv"], OT, memT, 512, fin_vx, pumps=2)
        flush()
        start2 = fence()

        QT2 = W[:, 0:2048].rearrange("p (h n) -> p h n", h=8)
        KT2 = W[:, 2048:4096].rearrange("p (h n) -> p h n", h=8)
        V2 = W[:, 4096:6144].rearrange("p (t n) -> p t n", t=2)
        U2 = W[:, 6144:8432].rearrange("p (f n) -> p f n", f=8)
        YC = W[:, 8432:10480].rearrange("p (f n) -> p f n", f=8)
        QI = W[:, 12784:13808].rearrange("p (f n) -> p f n", f=4)
        KI = W[:, 13808:14064]
        SG = W[:, 14064:14576].rearrange("p (i n) -> p i n", i=2)
        SC = W[:, 14832:15216]
        BG = W[:, 15728:16240]
        WI = ST[:, 496:512]
        qi_tok, q2_tok, k2_tok, v2_tok = {}, {}, {}, {}

        def fin_cols(dst, toks_, i, *tokens):
            def fin(f, L, R, tok):
                toks_[4 * i + f] = join(dst[:, 4 * i + f, :], L, R, tok, *tokens)
                return toks_[4 * i + f]
            return fin

        cols_group(G["b2_qi"], XT, xt, fin_cols(QI, qi_tok, 0, start2))

        u = G["b2_ki"][0]
        bk, rk = take("main")
        bw, rw = take("main")
        ki_tok = {}

        def fn_ki(h, l, tokens):
            for k in range(8):
                a = k * 512
                mm(PB[bk][:, :], h[:, k, 0:128], XT[:, a:a + 512], k == 0, False, tokens, xt[k], rk)
                last = mm(PB[bk][:, 0:256], l[:, k, 0:128], XT[:, a:a + 256], False, k == 7, done=(k == 7))
            ki_tok["k"] = join(KI, PB[bk][:, 0:256], PB[bk][:, 256:512], last, start2)
            give("main", bk, ki_tok["k"])
            for t in range(2):
                for k in range(8):
                    a = k * 512 + t * P
                    o = PB[bw][:, 8 * t:8 * t + 8]
                    mm(o, XT[:, a:a + P], h[:, k, 128:136], k == 0 and t == 0, False, rw)
                    mm(o, XT[:, a:a + P], l[:, k, 128:136], False, False)
                    last = mm(o, XT[:, a + 256:a + 256 + P], h[:, k, 128:136], False, k == 7 and t == 1,
                              done=(k == 7 and t == 1))
            ki_tok["w"] = act(partial(nc.scalar.activation, WI, PB[bw][:, 0:16], ACT.Copy, scale=8.0 ** -0.5), last)
            give("main", bw, ki_tok["w"])
            return last

        use(u, fn_ki)

        sel_tok, sel_free = {}, {}

        def index_side():
            acc = None
            for h in range(8):
                while not free["aux"]:
                    yield
                r0 = 64 * (h % 2)
                bank, tk = head_scores(QI[r0:r0 + 64, h // 2, :], KI[r0:r0 + 64, :], qi_tok[h // 2], ki_tok["k"])
                i = ring_at[0] % 3
                ring_at[0] += 1
                r = SP_[:, i, :]
                a = act(partial(nc.scalar.activation, r, PB[bank][:, 0:384], ACT.Relu, scale=0.125),
                        tk, sp_free[i])
                give("aux", bank, a)
                base = causal if h == 0 else SC
                for t, (c0, c1) in enumerate(((0, 128), (128, 384))):
                    acc = dve(partial(nc.vector.scalar_tensor_tensor, 
                        out=SC[:, c0:c1], in0=r[:, c0:c1], scalar=WI[:, 8 * t + h:8 * t + h + 1],
                        in1=base[:, c0:c1], op0=ALU.mult, op1=ALU.add), a, ki_tok["w"], acc, start2)
                sp_free[i] = acc
                if h % 2:
                    yield
            last = {0: acc, 1: acc}
            for rnd in range(8):
                ms = []
                for t, (c0, c1) in enumerate(((0, 128), (128, 384))):
                    m8 = stat(8)
                    ms.append((m8, dve(partial(nc.vector.max, m8, SC[:, c0:c1]), last[t])))
                for t, (c0, c1) in enumerate(((0, 128), (128, 384))):
                    m8, tk = ms[t]
                    last[t] = dve(partial(nc.vector.match_replace, 
                        out=SC[:, c0:c1], in_to_replace=m8, in_values=SC[:, c0:c1], imm_value=-3e38), tk)
                yield
            a = dve(partial(nc.vector.tensor_scalar, SC, SC, -2e38, NEG, ALU.is_gt, ALU.mult), last[0], last[1])
            sel_tok[0] = dve(partial(nc.vector.tensor_tensor, SC, SC, causal, ALU.add), a)

        side.append(index_side())

        sg_free = [None, None]
        sg_tok = {}
        u2z = dve(partial(nc.vector.memset, U2[:, :, 0:30], 0.0), start2)
        u2_tok = {}
        SGv = W[:, 8432:9456].rearrange("p (f n) -> p f n", f=4)
        SG4 = ZT[:, 0:1024]

        def fin_cg(i):
            def fin(f, L, R, tok):
                d = join(GS[:, f, :], L, R, tok, gs_free.get(f), start2)
                sg_tok[f] = act(partial(nc.scalar.activation, GS[:, f, :], GS[:, f, :], ACT.Sigmoid), d)
                return d
            return fin

        GS = W[:, 4096:5120].rearrange("p (f n) -> p f n", f=4)
        gs_free = {}

        def fin_ca(i):
            def fin(f, L, R, tok):
                u_ = U2[:, 4 * i + f, 30:286]
                d = join(u_, L, R, tok, start2)
                u2_tok[4 * i + f] = gs_free[f] = dve(
                    partial(nc.vector.tensor_tensor, u_, u_, GS[:, f, :], ALU.mult), d, sg_tok[f])
                return d
            return fin

        zc_tok = {}
        conv_done = [False]

        def conv_side():
            y = {}
            for f in range(8):
                while f not in u2_tok:
                    yield
                d = dve(partial(nc.vector.tensor_scalar, YC[:, f, :], U2[:, f, 0:256], prm("convw2", f), prm("convb2", f),
                                                       ALU.mult, ALU.add), u2_tok[f], u2z, start2)
                for k in range(1, 31):
                    d = dve(partial(nc.vector.scalar_tensor_tensor, 
                        out=YC[:, f, :], in0=U2[:, f, k:k + 256], scalar=prm("convw2", 8 * k + f), in1=YC[:, f, :],
                        op0=ALU.mult, op1=ALU.add), d)
                    if k % 8 == 0:
                        yield
                y[f] = d
                yield
            conv_done[0] = fence()
            yall = W[:, 8432:10480]
            while not free["aux"]:
                yield
            bank, rel = take("aux")
            for f in range(8):
                tk = mm(PB[bank][:, 0:256], ones, YC[:, f, :], f == 0, f == 7, y[f], rel, done=(f == 7))
            mu = U2[:, 0, 0:256]
            m = act(partial(nc.scalar.activation, mu, PB[bank][:, 0:256], ACT.Copy, scale=1.0 / D), tk, conv_done[0])
            give("aux", bank, m)
            yield
            c = dve(partial(nc.vector.tensor_tensor, YC, YC, mu.unsqueeze(1).broadcast_to([P, 8, 256]), ALU.subtract), m)
            sqs = W[:, 6144 + 286:6144 + 286 + 512].rearrange("p (i n) -> p i n", i=2)
            yield
            while not free["aux"]:
                yield
            bank, rel = take("aux")
            fr = [None, None]
            for f in range(8):
                q = sqs[:, f % 2, :]
                a = act(partial(nc.scalar.activation, q, YC[:, f, :], ACT.Square), c, fr[f % 2])
                fr[f % 2] = tk = mm(PB[bank][:, 0:256], ones, q, f == 0, f == 7, a, rel, done=True)
                if f % 4 == 3:
                    yield
            v, r = U2[:, 4, 0:256], U2[:, 5, 0:256]
            a = dve(partial(nc.vector.tensor_scalar, v, PB[bank][:, 0:256], 1.0 / D, EPS, ALU.mult, ALU.add), tk)
            give("aux", bank, a)
            b = act(partial(nc.scalar.activation, v, v, ACT.Sqrt), a)
            r_t = dve(partial(nc.vector.reciprocal, r, v), b)
            c = dve(partial(nc.vector.tensor_tensor, YC, YC, r.unsqueeze(1).broadcast_to([P, 8, 256]), ALU.mult), r_t)
            yield
            ss = [act(partial(nc.scalar.activation, YC[:, f, :], YC[:, f, :], ACT.Silu, scale=prm("lng", f),
                                                  bias=prm("lnb", f)), c) for f in range(8)]
            for f in range(8):
                zc_tok[f] = halves(ZT[:, f * 512:f * 512 + 512], YC[:, f, :], ss[f], start2)
            yield
            conv_done.append(fence())

        for i in range(2):
            cols_group(G[f"b2_cg{i}"], XT, xt, fin_cg(i))
            cols_group(G[f"b2_ca{i}"], XT, xt, fin_ca(i))
            if i == 0:
                side.append(conv_side())
        gs_end = fence()
        for i in range(2):
            cols_group(G[f"b2_k{i}"], XT, xt, fin_cols(KT2, k2_tok, i, start2))
        for i in range(2):
            cols_group(G[f"b2_q{i}"], XT, xt, fin_cols(QT2, q2_tok, i, start2))

        def fin_v(i):
            def fin(t, bank, tok):
                v2_tok[i, t] = act(partial(nc.scalar.activation, V2[:, t, 512 * i:512 * i + 512], bank, ACT.Copy), tok, gs_end)
                return v2_tok[i, t]
            return fin

        for i in range(2):
            rows_group(G[f"b2_v{i}"], XT, xt, 512, fin_v(i))

        o2_tok = {}

        def dsa_side():
            while 0 not in sel_tok:
                yield

            def item(h):
                while not free["aux"]:
                    yield
                bank, tk = head_scores(QT2[:, h, :], KT2[:, h, :], q2_tok[h], k2_tok[h])
                for v in head_softmax(bank, tk, SC, 128.0 ** -0.5, 1.0, None, sel_tok[0]):
                    if v is None:
                        yield
                i, tk = v
                yield
                while not free["aux"]:
                    yield
                c = head_PT(i, tk)
                yield
                while not free["aux"]:
                    yield
                bank, rel = take("aux")
                o = PB[bank]
                mm(o[:, 0:256], V2[:, 0, h * P:h * P + P], PT[:, i, 0:256], True, False, c, rel, v2_tok[h // 4, 0])
                pt_free[i] = mm(o[:, 128:256], V2[:, 1, h * P:h * P + P], PT[:, i, 256:384], False, True,
                                v2_tok[h // 4, 1], done=True)
                yield
                o2_tok[h] = bank_halves(h, bank, pt_free[i])

            yield from in_flight(8, item, lambda h: None)

        side.append(dsa_side())

        GA2 = W[:, 12784:14832].rearrange("p (t n) -> p t n", t=2)
        GC2 = W[:, 6144:8192].rearrange("p (t n) -> p t n", t=2)
        while 0 not in sel_tok:
            pump()
        idx_end = fence()
        raw_tok = {}
        bg_free = [None]

        def gate_group(name, i, dst, off, *tokens):
            bt = dma(BG, A["b_gate_2"][:, off + 512 * i:off + 512 * i + 512].broadcast_to([P, 512]), bg_free[0], start2)

            def fin(t, bank, tok):
                r = dve(partial(nc.vector.tensor_tensor, dst[:, t, 512 * i:512 * i + 512], bank, BG, ALU.add), tok, bt, *tokens)
                raw_tok[name, i, t] = bg_free[0] = r
                return r
            rows_group(G[f"b2_{name}{i}"], XT, xt, 512, fin, pumps=2)

        for i in range(2):
            gate_group("ga", i, GA2, 1024, idx_end)
        while len(conv_done) < 2:
            pump()
        conv_end = conv_done[1]
        for i in range(2):
            gate_group("gc", i, GC2, 0, conv_end)
        flush()
        end2 = fence()
        g2 = {}
        for nm, G_ in (("ga", GA2), ("gc", GC2)):
            for t in range(2):
                g2[nm, t] = act(partial(nc.scalar.activation, G_[:, t, :], G_[:, t, :], ACT.Sigmoid),
                                raw_tok[nm, 0, t], raw_tok[nm, 1, t])
        MX2 = W[:, 0:2048]
        MX2v = MX2.rearrange("p (t n) -> p t n", t=2)
        TM2 = W[:, 2048:4096].rearrange("p (i n) -> p i n", i=4)
        m2 = {}

        def fin_wa(i):
            def fin(t, bank, tok):
                m2[i, t] = dve(partial(nc.vector.tensor_tensor, MX2v[:, t, 512 * i:512 * i + 512], bank,
                                                         GA2[:, t, 512 * i:512 * i + 512], ALU.mult),
                               tok, g2["ga", t], end2)
                return m2[i, t]
            return fin

        def fin_wc(i):
            def fin(t, bank, tok):
                x = TM2[:, 2 * i + t, :]
                r = dve(partial(nc.vector.tensor_tensor, x, bank, GC2[:, t, 512 * i:512 * i + 512], ALU.mult),
                        tok, g2["gc", t], end2)
                m = MX2v[:, t, 512 * i:512 * i + 512]
                m2[i, t] = dve(partial(nc.vector.tensor_tensor, m, m, x, ALU.add), r, m2[i, t])
                return r
            return fin

        for i in range(2):
            rows_group(G[f"b2_wa{i}"], OT, o2_tok, 512, fin_wa(i))
        for i in range(2):
            rows_group(G[f"b2_wc{i}"], ZT, zc_tok, 512, fin_wc(i))
        xfree = pe.last()
        mt = drain(to_T(MX2, [[m2[0, t], m2[1, t]] for t in range(2)], XT, None, xfree))
        for i in range(2):
            rows_group(G[f"b2_wm{i}"], XT, mt, 512, fin_add(i))

        xt = drain(norm_to_XT("normx"))
        QX = W[:, 0:1024].rearrange("p (h n) -> p h n", h=4)
        S5 = W[:, 1024:2048].rearrange("p (i n) -> p i n", i=2)
        P5 = W[:, 2048:3072].rearrange("p (i n) -> p i n", i=2)
        qx_tok, ox_tok = {}, {}
        cols_group(G["xq"], XT, xt, fin_cols(QX, qx_tok, 0, fence()))
        s5_free, p5_free = [None, None], [None, None]
        XSC = 128.0 ** -0.5

        def cross_item(h):
            while not free["aux"]:
                yield
            bank, rel = take("aux")
            o = PB[bank]
            for t in range(2):
                tk = mm(o[:, 256 * t:256 * t + 256], QX[:, h, t * P:t * P + P], KXT[:, h, :], t == 0, t == 1,
                        rel, qx_tok[h], kx_tok[h], done=(t == 1))
            i = h % 2
            s = S5[:, i, :]
            m, nm, sm, ri = stat(2), stat(2), stat(2), stat(2)
            a = dve(partial(nc.vector.tensor_reduce, m, o[:, :].rearrange("p (t n) -> p t n", t=2), AX.X, ALU.max), tk)
            b = dve(partial(nc.vector.tensor_scalar, nm, m, -XSC, None, ALU.mult), a)
            for t in range(2):
                c = act(partial(nc.scalar.activation, s[:, 256 * t:256 * t + 256], o[:, 256 * t:256 * t + 256], ACT.Exp,
                                                    bias=nm[:, t:t + 1], scale=XSC, accum_out=sm[:, t:t + 1]),
                        b, s5_free[i])
            give("aux", bank, c)
            yield
            f = dve(partial(nc.vector.reciprocal, ri, sm), c)
            for t in range(2):
                g = dve(partial(nc.vector.tensor_scalar, s[:, 256 * t:256 * t + 256], s[:, 256 * t:256 * t + 256],
                                                       ri[:, t:t + 1], None, ALU.mult), f)
            yield
            while not free["aux"]:
                yield
            bank2, rel = take("aux")
            o2 = PB[bank2]
            for k in range(2):
                for t in range(2):
                    tk = pe(partial(nc.tensor.transpose, o2[:, 256 * k + P * t:256 * k + P * t + P],
                                                            s[:, 256 * t + P * k:256 * t + P * k + P], ident),
                            g, rel, done=(k == 1 and t == 1))
            s5_free[i] = tk
            c = act(partial(nc.scalar.activation, P5[:, i, :], o2[:, :], ACT.Copy), tk, p5_free[i])
            give("aux", bank2, c)
            yield
            while not free["aux"]:
                yield
            bank3, rel = take("aux")
            o3 = PB[bank3]
            for k in range(2):
                tk = mm(o3[:, 0:256], VX[:, k, h * P:h * P + P], P5[:, i, 256 * k:256 * k + 256], k == 0, k == 1,
                        c, rel, vx_tok[k], done=(k == 1))
            p5_free[i] = tk
            ox_tok[h] = bank_halves(h, bank3, tk)

        for _ in in_flight(4, cross_item, lambda h: None):
            pass
        for i in range(2):
            rows_group(G[f"xo{i}"], OT, ox_tok, 512, fin_add(i))
        ht = drain(norm_to_XT("normffn"))
        GF = W[:, 0:1024]
        gf_tok = dma(GF, A["norm_final_g_2"].broadcast_to([P, D]), fence())
        ffn("f2", ht)

        n = norm_rows(X, XS, SQB, x_toks())
        outv = out.rearrange("o (t p) d -> p (o t) d", p=P)
        s_out = sem("stored")
        for t in range(2):
            o = XS[:, t * D:t * D + D]
            f = dve(partial(nc.vector.tensor_tensor, o, o, GF, ALU.mult), n[t], gf_tok)
            sp.wait(f)
            sp.queue.append(partial(signalling, partial(nc.sync.dma_start, outv[:, t, :], o), s_out, 16))
        sp.wait((s_out, 32))

        block = ctx.enter_context(nc.Block())

        @block.sync
        def _(e):
            for f in sp.queue:
                f()

        @block.tensor
        def _(e):
            for f in pe.queue:
                f()

        @block.scalar
        def _(e):
            for f in act.queue:
                f()

        @block.vector
        def _(e):
            for f in dve.queue:
                f()

        @block.gpsimd
        def _(e):
            for f in pool.queue:
                f()


def constants():
    c = np.zeros((P, CS["end"]), np.float32)
    c[:, 0:128] = np.eye(P)
    c[:, 128:256] = 1.0
    q, k = np.arange(P)[:, None], np.arange(2 * P)[None, :]
    for c0, t, n in ((0, 0, 128), (128, 1, 256)):
        d = (q + P * t - k[:, :n]).astype(np.float32)
        c[:, CS["dist"] + c0:CS["dist"] + c0 + n] = np.where(d >= 0, -d, -1e33)
        c[:, CS["causal"] + c0:CS["causal"] + c0 + n] = np.where(d >= 0, 0, NEG)
    c2 = np.zeros((P, C2["end"]), np.float32)
    b = c2[:, 0:480].reshape(P, 2, 8, 2, 15)
    m = c2[:, 480:960].reshape(P, 2, 8, 2, 15)
    cend = 16 * np.arange(15) + 31
    b[:] = NEG
    for t in range(2):
        d = (np.arange(P)[:, None] + P * t - cend[None, :]).astype(np.float32)
        for h in range(8):
            slope = np.float32(2.0 ** -(h + 1))
            b[:, t, h, h // 4] = np.where(d >= 0, -slope * d, NEG)
            m[:, t, h, h // 4] = d >= 0
    return c, c2


def kernel(**inputs):
    import concourse.bacc as bacc
    from concourse.bass_utils import run_bass_kernel_spmd

    I = {k: np.asarray(v) for k, v in inputs.items()}
    params = np.zeros((P, NPRM), np.float32)

    def tiles(v):
        return v.reshape(-1, 8, P).transpose(2, 0, 1).reshape(P, -1)

    for name, key in (("norm1", "norm1_g"), ("norm2", "norm2_g"), ("convw", "conv_w"), ("normmix", "norm_mix_g_2"),
                      ("convw2", "conv_w_2"), ("convb2", "conv_b_2"), ("lng", "conv_ln_g_2"), ("lnb", "conv_ln_b_2"),
                      ("normx", "norm_x_g_2"), ("normmem", "norm_mem_g_2"), ("normffn", "norm_ffn_g_2")):
        v = tiles(I[key].reshape(-1, D))
        params[:, PRM[name]:PRM[name] + v.shape[1]] = v
    params[0:64, PRM["qg"]] = I["q_norm_g"][0]
    params[0:64, PRM["kg"]:PRM["kg"] + 3] = I["k_norm_g"][0].T
    params[0:64, PRM["posk"]:PRM["posk"] + 32] = I["cmp_pos_k"][0].T
    params[0:64, PRM["posv"]:PRM["posv"] + 32] = I["cmp_pos_v"][0].T
    wcmp = np.concatenate([I[k][0].reshape(32, 64, 64).transpose(1, 0, 2).reshape(64, 2048)
                           for k in ("w_cmp_k", "w_cmp_v")], axis=1)
    c, c2 = constants()
    arrays = {"params": params, "consts": c, "consts2": c2, "wcmp": wcmp, "x": I["x"], "mem_2": I["mem_2"],
              "b_gate_2": I["b_gate_2"], "norm_final_g_2": I["norm_final_g_2"].reshape(1, D)}
    for k in ("w_in", "w_branch_a", "w_branch_b", "w_out", "w_up", "w_down", "w_in_2", "w_conv_out_2",
              "w_attn_out_2", "w_mix_out_2", "wx_q_2", "wx_kv_2", "wx_o_2", "w_ff1_2", "w_ff2_2"):
        arrays[k] = I[k][0]
    nc = bacc.Bacc("TRN2", target_bir_lowering=False, num_devices=1)
    arrays = {k: np.ascontiguousarray(v) for k, v in arrays.items()}
    A = {k: nc.dram_tensor(f"in_{k}", v.shape, mybir.dt.from_np(v.dtype), kind="ExternalInput").ap()
         for k, v in arrays.items()}
    out = nc.dram_tensor("out_0", (1, 256, D), F32, kind="ExternalOutput").ap()
    build(nc, A, out)
    r = run_bass_kernel_spmd(nc, [{f"in_{k}": v for k, v in arrays.items()}], core_ids=[0])
    return r.results[0]["out_0"]
```

```python
from contextlib import ExitStack

from functools import partial

import numpy as np

import concourse.bass as bass
from concourse import mybir

F32 = mybir.dt.float32
F32R = mybir.dt.float32r
ALU = mybir.AluOpType
ACT = mybir.ActivationFunctionType
AX = mybir.AxisListType

P = 128
D = 1024
UC = 1024
NRAW = 5
PE_CONV = 6
STEPS, EARLY = 8, 0
SLACK = 4500
NW = 5
EPS = 1e-6
NEG = -1e30

PRM = {}
_n = 0
for _name, _w in (("norm1", 8), ("norm2", 8), ("convw", 24), ("normmix", 8), ("convw2", 248), ("convb2", 8),
                  ("lng", 8), ("lnb", 8), ("normx", 8), ("normmem", 8), ("normffn", 8), ("qg", 1), ("kg", 3),
                  ("posk", 32), ("posv", 32)):
    PRM[_name] = _n
    _n += _w
NPRM = _n
CS = {"ident": 0, "ones": 128, "dist": 256, "causal": 640, "mhalf": 1024, "end": 1025}
C2 = {"cbias": 0, "cmask": 480, "end": 960}


def signalling(fn, sem, n):
    fn().then_inc(sem, n)


def columns(a):
    n = 1
    for k in a.shape[1:]:
        n *= k
    return n


class Engine:

    def __init__(self, eng, sem, fixed=60, per_column=1.0):
        self.eng, self.sem, self.count, self.seen, self.queue = eng, sem, 0, {}, []
        self.fixed, self.per_column, self.clock = fixed, per_column, 0

    def wait(self, *tokens):
        for t in tokens:
            if t is None:
                continue
            if isinstance(t, list):
                self.wait(*t)
                continue
            sem, val = t[0], t[1]
            self.clock = max(self.clock, t[2])
            if self.seen.get(sem.name, 0) < val:
                self.seen[sem.name] = val
                self.queue.append(partial(self.eng.wait_ge, sem, val))

    def __call__(self, fn, *tokens, done=True, passes=1):
        self.wait(*tokens)
        aps = [a for a in list(fn.args) + list(fn.keywords.values()) if isinstance(a, bass.AP)]
        self.clock += self.fixed + self.per_column * passes * max(columns(a) for a in aps)
        if not done:
            self.queue.append(fn)
            return None
        self.count += 1
        self.queue.append(partial(signalling, fn, self.sem, 1))
        return (self.sem, self.count, self.clock + 130)

    def last(self):
        return (self.sem, self.count, self.clock) if self.count else None


def when(t):
    if t is None:
        return 0
    if isinstance(t, list):
        return max([when(x) for x in t] + [0])
    return t[2]


def build(nc, A, out):
    ctx = ExitStack()
    with ctx:
        def sb(name, cols, dt=F32):
            return ctx.enter_context(nc.sbuf_tensor(name, [P, cols], dt))

        def sem(name):
            return ctx.enter_context(nc.semaphore(name))

        raw = [sb(f"raw{i}", UC) for i in range(NRAW)]
        whi = [sb(f"whi{i}", UC, F32R) for i in range(NW)]
        wlo = [sb(f"wlo{i}", UC, F32R) for i in range(NW)]
        XT = sb("XT", 8 * 512, F32R)
        ZT = sb("ZT", 8 * 512, F32R)
        OT = sb("OT", 8 * 512, F32R)
        X = sb("X", 2 * D)
        CST = sb("CST", CS["end"])
        PR = sb("PR", NPRM)
        KV = sb("KV", 2048)
        ST = sb("ST", 512)
        W = sb("W", 18288)
        DG = sb("DG", 4 * P)
        PB = [ctx.enter_context(nc.psum_tensor(f"pb{i}", [P, 512], F32)) for i in range(8)]

        pe = Engine(nc.tensor, sem("done_pe"), 0, 1 / 2.4)
        act = Engine(nc.scalar, sem("done_act"), 230, 0.84)
        dve = Engine(nc.vector, sem("done_dve"), 90, 1.05)
        pool = Engine(nc.gpsimd, sem("done_pool"), 400, 160)
        sp = Engine(nc.sync, sem("done_sp"))
        s_raw = [sem(f"raw_landed{i}") for i in range(NRAW)]
        n_raw = [0] * NRAW
        sems = [0]

        def dma(dst, src, *tokens):
            s = sem(f"load{sems[0]}")
            sems[0] += 1
            sp.wait(*tokens)
            sp.queue.append(partial(signalling, partial(nc.sync.dma_start, dst, src), s, 16))
            return (s, 16, 0)

        def fence():
            return [e.last() for e in (pe, act, dve, pool)]

        ident = CST[:, 0:128]
        ones = CST[:, 128:256]
        distb = CST[:, 256:640]
        causal = CST[:, 640:1024]

        def prm(name, i=0, n=1, rows=P):
            return PR[0:rows, PRM[name] + i:PRM[name] + i + n]

        st_at = [0]

        def stat(n):
            if st_at[0] + n > 496:
                st_at[0] = 0
            a = st_at[0]
            st_at[0] += n
            return ST[:, a:a + n]

        keep_at = [960]

        def keep(n):
            keep_at[0] += n
            assert keep_at[0] <= 2048
            return KV[:, keep_at[0] - n:keep_at[0]]

        free = {"main": [(b, None) for b in range(4)], "aux": [(b, None) for b in range(4, 8)]}

        def take(kind):
            return free[kind].pop(0)

        def give(kind, bank, *tokens):
            free[kind].append((bank, list(tokens)))

        units = []
        landed, split_hi, split_lo, used = {}, {}, {}, {}

        def unit_rows(w, kt0, nk, n0, n):
            units.append((w[kt0 * P:(kt0 + nk) * P, n0:n0 + n].rearrange("(k p) n -> p k n", p=P), nk, n))
            return len(units) - 1

        def load(u):
            if u >= len(units):
                return
            src, nk, n = units[u]
            i = u % NRAW
            if u >= NRAW:
                sp.wait(split_lo[u - NRAW])
            parts = src if isinstance(src, list) else [(src, 0, n)]
            view = raw[i][:, 0:nk * n].rearrange("p (k n) -> p k n", k=nk)
            for s, c0, w in parts:
                n_raw[i] += 16
                sp.queue.append(partial(signalling, partial(nc.sync.dma_start, view[:, :, c0:c0 + w], s), s_raw[i], 16))
            landed[u] = (s_raw[i], n_raw[i], sp.clock)

        split_at = [0]

        def split(u):
            _, nk, n = units[u]
            c = nk * n
            r, h, l = raw[u % NRAW][:, 0:c], whi[u % NW][:, 0:c], wlo[u % NW][:, 0:c]
            split_hi[u] = act(partial(nc.scalar.activation, h, r, ACT.Copy), landed[u], used.get(u - NW))
            split_lo[u] = dve(partial(nc.vector.tensor_tensor, l, r, h.bitcast(F32), ALU.subtract), split_hi[u])
            load(u + NRAW)

        side = []

        def add_side(gen, first=True, uses=None):
            side.insert(0 if first else len(side), [gen, None, uses or (dve, act)])

        def step(c):
            c[1] = next(c[0], StopIteration)
            if c[1] is StopIteration:
                side.remove(c)

        def pump():
            for c in list(side):
                for _ in range(STEPS):
                    if c not in side or when(c[1]) > pe.clock + EARLY or \
                            max(e.clock for e in c[2]) > pe.clock + SLACK:
                        break
                    step(c)
                    if c[1] is None:
                        break

        def turn():
            for c in sorted(side, key=lambda c: when(c[1])):
                step(c)

        def flush():
            k = 0
            while side:
                turn()
                k += 1
                assert k < 2000

        spread = []

        def use(u, fn):
            assert u == len(used)
            while split_at[0] < min(u + NW, len(units)):
                split(split_at[0])
                split_at[0] += 1
            _, nk, n = units[u]
            h = whi[u % NW][:, 0:nk * n].rearrange("p (k n) -> p k n", k=nk)
            l = wlo[u % NW][:, 0:nk * n].rearrange("p (k n) -> p k n", k=nk)
            used[u] = fn(h, l, [split_hi[u], split_lo[u]])
            if spread:
                spread.pop(0)()
            pump()

        def mm(o, l, r, start, stop, *tokens, done=False):
            return pe(partial(nc.tensor.matmul, o, l, r, start=start, stop=stop, skip_group_check=True), *tokens, done=done,
                      passes=4 if r.dtype == F32 else 1)

        def rows_group(us, T, toks, n, finish):
            banks = [take("main") for _ in range(2)]
            nks = sum(units[u][1] for u in us)
            kt = 0
            for u in us:
                def fn(h, l, tokens):
                    nonlocal kt
                    nk = units[u][1]
                    pairs = [(k, t) for k in range(nk) for t in range(2)]
                    if kt + nk == nks:
                        pairs = [(k, t) for t in range(2) for k in range(nk)]
                    for k, t in pairs:
                        o = PB[banks[t][0]][:, 0:n]
                        a = (kt + k) * 512 + t * P
                        fin = kt + k == nks - 1
                        mm(o, T[:, a:a + P], h[:, k, :], kt + k == 0, False, tokens, toks[kt + k], banks[t][1])
                        mm(o, T[:, a:a + P], l[:, k, :], False, False)
                        last = mm(o, T[:, a + 256:a + 256 + P], h[:, k, :], False, fin,
                                  done=fin or (k, t) == pairs[-1])
                        if fin:
                            got[t] = last
                    kt += nk
                    return last
                got = {}
                use(u, fn)
            for t in range(2):
                rel = finish(t, PB[banks[t][0]][:, 0:n], got[t])
                give("main", banks[t][0], rel)

        def cols_group(us, T, toks, finish, nf=4):
            banks = [take("main") for _ in range(nf)]
            kt = 0
            got = {}
            for i, u in enumerate(us):
                def fn(h, l, tokens):
                    nk = units[u][1]
                    for f in range(nf):
                        o = PB[banks[f][0]]
                        for k in range(nk):
                            a = (kt + k) * 512
                            mm(o[:, :], h[:, k, f * P:f * P + P], T[:, a:a + 512], kt + k == 0, False,
                               tokens, toks[kt + k], banks[f][1])
                            fin = i == len(us) - 1 and k == nk - 1
                            last = mm(o[:, 0:256], l[:, k, f * P:f * P + P], T[:, a:a + 256], False, fin,
                                      done=fin or (k == nk - 1 and f == nf - 1))
                        if i == len(us) - 1:
                            got[f] = last
                            rel = finish(f, o[:, 0:256], o[:, 256:512], last)
                            give("main", banks[f][0], rel)
                    while later:
                        later.pop(0)()
                    return last
                use(u, fn)
                kt += units[u][1]

        later = []
        rt_at = [0]
        RT = W[:, 15216:15728].rearrange("p (i n) -> p i n", i=2)
        rt_free = [None, None]

        def join(dst, L, R, tok, *tokens):
            i = rt_at[0] % 2
            rt_at[0] += 1
            a = act(partial(nc.scalar.activation, RT[:, i, :], R, ACT.Copy), tok, rt_free[i])
            d = dve(partial(nc.vector.tensor_tensor, dst, L, RT[:, i, :], ALU.add), a, *tokens)
            rt_free[i] = d
            return d

        def halves(dst, src, *tokens):
            h = act(partial(nc.scalar.activation, dst[:, 0:256], src, ACT.Copy), *tokens)
            return dve(partial(nc.vector.tensor_tensor, dst[:, 256:512], src, dst[:, 0:256].bitcast(F32), ALU.subtract), h)

        def rsqrt(dst, src, scale, *tokens):
            n = src.shape[1]
            rows = src.shape[0]
            a = stat(n)[0:rows, :]
            t = dve(partial(nc.vector.tensor_scalar, a, src, scale, EPS, ALU.mult, ALU.add), *tokens)
            half = CST[0:rows, CS["mhalf"]:CS["mhalf"] + 1].broadcast_to([rows, n])
            return pool(partial(nc.gpsimd.tensor_tensor, dst, a, half, ALU.pow), t, const_tok)

        def to_T(out_tok, src, toks, dst, gain, *tokens):
            for j in range(4):
                while not free["aux"]:
                    yield
                bank, rel = take("aux")
                for k in range(2):
                    for t in range(2):
                        s = src[:, t * D + (2 * j + k) * P:t * D + (2 * j + k) * P + P]
                        o = PB[bank][:, k * 256 + t * P:k * 256 + t * P + P]
                        tt = pe(partial(nc.tensor.transpose, o, s, ident), toks[t][j // 2], rel, const_tok,
                                done=(k == 1 and t == 1))
                if gain is None:
                    b = PB[bank][:, :].rearrange("p (k n) -> p k n", k=2)
                    d = dst[:, 2 * j * 512:(2 * j + 2) * 512].rearrange("p (k h n) -> p k h n", k=2, h=2)
                    h = act(partial(nc.scalar.activation, d[:, :, 0, :], b, ACT.Copy), tt, *tokens)
                    l = dve(partial(nc.vector.tensor_tensor, d[:, :, 1, :], b, d[:, :, 0, :].bitcast(F32),
                                                                ALU.subtract), h, *tokens)
                    out_tok[2 * j] = out_tok[2 * j + 1] = [h, l]
                else:
                    hs = []
                    for k in range(2):
                        kt = 2 * j + k
                        b = PB[bank][:, k * 256:k * 256 + 256]
                        g = prm(gain, kt)
                        h = act(partial(nc.scalar.activation, dst[:, kt * 512:kt * 512 + 256], b, ACT.Copy,
                                                                       scale=g), tt, *tokens)
                        hs.append(h)
                    for k in range(2):
                        kt = 2 * j + k
                        b = PB[bank][:, k * 256:k * 256 + 256]
                        g = prm(gain, kt)
                        l = dve(partial(nc.vector.scalar_tensor_tensor, 
                            out=dst[:, kt * 512 + 256:kt * 512 + 512], in0=b, scalar=g,
                            in1=dst[:, kt * 512:kt * 512 + 256].bitcast(F32), op0=ALU.mult, op1=ALU.subtract),
                            hs[1], *tokens)
                        out_tok[kt] = [hs[k], l]
                give("aux", bank, out_tok[2 * j], out_tok[2 * j + 1])
                yield []

        def drain(g):
            for _ in g:
                pass

        def norm_rows(src, dst, sq, src_toks, *tokens, gain=None):
            parts, rs = {}, []
            for i in range(2):
                a = None
                for t in range(2):
                    parts[t, i] = stat(1)
                    a = act(partial(nc.scalar.activation, sq[:, 512 * i:512 * i + 512],
                                    src[:, t * D + 512 * i:t * D + 512 * i + 512], ACT.Square, accum_out=parts[t, i]),
                            src_toks[t][i], a, *tokens)
                    if i == 1:
                        rs.append(a)
            out_t = [[], []]
            for t in range(2):
                ss, r = stat(1), stat(1)
                b = dve(partial(nc.vector.tensor_tensor, ss, parts[t, 0], parts[t, 1], ALU.add), rs[t])
                rs[t] = (r, rsqrt(r, ss, 1.0 / D, b))
            for i in range(2):
                for t in range(2):
                    r, tk = rs[t]
                    c = slice(t * D + 512 * i, t * D + 512 * i + 512)
                    if gain is None:
                        f = partial(nc.vector.tensor_scalar, dst[:, c], src[:, c], r, None, ALU.mult)
                    else:
                        f = partial(nc.vector.scalar_tensor_tensor, out=dst[:, c], in0=src[:, c], scalar=r,
                                    in1=gain[:, 512 * i:512 * i + 512], op0=ALU.mult, op1=ALU.mult)
                    out_t[t].append(dve(f, tk, *tokens))
            return out_t

        w_in, w_in2 = A["w_in"], A["w_in_2"]
        G = {}

        def rows_units(name, w, n0, n, kts=8, kt0=0):
            G[name] = [unit_rows(w, kt0 + k, 2, n0, n) for k in range(0, kts, 2)]

        rows_units("b1_q", w_in, 0, 512)
        rows_units("b1_kv", w_in, 512, 512)
        rows_units("b1_w", w_in, 1024, 280)
        for i in range(2):
            for nm, o in (("c", 2328), ("x", 3352), ("b", 1304)):
                rows_units(f"b1_{nm}{i}", w_in, o + 512 * i, 512)
        for nm, o in (("gb", 5400), ("ga", 4376)):
            for i in range(2):
                rows_units(f"b1_{nm}{i}", w_in, o + 512 * i, 512)
        for i in range(2):
            rows_units(f"b1_wb{i}", A["w_branch_b"], 512 * i, 512)
        for i in range(2):
            rows_units(f"b1_wa{i}", A["w_branch_a"], 512 * i, 512, 4)
        for i in range(2):
            rows_units(f"b1_wo{i}", A["w_out"], 512 * i, 512)
        rows_units("mk", A["wx_kv_2"], 0, 512)

        def ffn_units(tag, up, down):
            def dn(c):
                for i in range(2):
                    rows_units(f"{tag}_dn{c}_{i}", down, 512 * i, 512, 4, 4 * c)
            for c in range(8):
                rows_units(f"{tag}_up{c}", up, 512 * c, 512)
                if c:
                    dn(c - 1)
            dn(7)

        ffn_units("f1", A["w_up"], A["w_down"])
        rows_units("mv", A["wx_kv_2"], 512, 512)

        def c_units(i):
            rows_units(f"b2_cg{i}", w_in2, 1024 + 512 * i, 512)
            rows_units(f"b2_ca{i}", w_in2, 512 * i, 512)

        c_units(0)
        rows_units("b2_qi", w_in2, 5120, 512)
        ki = w_in2[:, 5632:5696].rearrange("(k p) n -> p k n", p=P)
        wi = w_in2[:, 5696:5704].rearrange("(k p) n -> p k n", p=P)
        units.append(([(ki, 0, 64), (ki, 64, 64)], 8, 128))
        units.append((wi, 8, 8))
        G["b2_ki"] = [len(units) - 2, len(units) - 1]
        c_units(1)
        for nm, o in (("k", 3072), ("q", 2048)):
            for i in range(2):
                rows_units(f"b2_{nm}{i}", w_in2, o + 512 * i, 512)
        for i in range(2):
            rows_units(f"b2_v{i}", w_in2, 4096 + 512 * i, 512)
        for nm, o in (("gc", 5704), ("ga", 6728)):
            for i in range(2):
                rows_units(f"b2_{nm}{i}", w_in2, o + 512 * i, 512)
        for i in range(2):
            rows_units(f"b2_wa{i}", A["w_attn_out_2"], 512 * i, 512)
        for i in range(2):
            rows_units(f"b2_wc{i}", A["w_conv_out_2"], 512 * i, 512)
        for i in range(2):
            rows_units(f"b2_wm{i}", A["w_mix_out_2"], 512 * i, 512)
        rows_units("xq", A["wx_q_2"], 0, 512)
        for i in range(2):
            rows_units(f"xo{i}", A["wx_o_2"], 512 * i, 512, 4)
        ffn_units("f2", A["w_ff1_2"], A["w_ff2_2"])

        xv = A["x"].rearrange("o (t p) d -> p (o t) d", p=P)
        x_tok = [dma(X[:, 0:D], xv[:, 0, :]), dma(X[:, D:2 * D], xv[:, 1, :])]
        const_tok = dma(CST[:, :], A["consts"])
        prm_tok = dma(PR[:, :], A["params"])
        for u in range(NRAW):
            load(u)
        c2_tok = dma(KV[:, 0:960], A["consts2"])
        cbias = KV[:, 0:480].rearrange("p (t n) -> p t n", t=2)
        cmask = KV[:, 480:960].rearrange("p (t n) -> p t n", t=2)

        QKV = W[:, 0:2608].rearrange("p (t n) -> p t n", t=2)
        TT = W[:, 2608:6704].rearrange("p (h n) -> p h n", h=16)
        WC = W[0:64, 6704:8752].rearrange("p (j e) -> p j e", j=32)
        PTC = W[0:30, 6704:8752].rearrange("p (h n) -> p h n", h=8)
        KP = W[0:64, 8752:9712].rearrange("p (b j) -> p b j", j=32)
        SP_ = [W[:, a:a + 384] for a in (10480, 10864, 11248, 9232)]
        PT = [W[:, a:a + 384] for a in (11632, 12016, 12400, 14840)]
        CC = W[:, 12784:13808].rearrange("p (f n) -> p f n", f=4)
        UU = W[:, 13808:14840].rearrange("p (f n) -> p f n", f=4)
        PC = W[:, 8752:9232].rearrange("p (t n) -> p t n", t=2)
        SQ = W[:, 2608:3632]

        wc_tok = dma(WC, A["wcmp"][:, 0:2048].rearrange("p (j e) -> p j e", j=32))

        SX = W[:, 4096:6144]
        n1 = norm_rows(X, SX, SQ, [[x, x] for x in x_tok])
        xt = {}
        drain(to_T(xt, SX, n1, XT, "norm1", prm_tok))
        early = fence()

        qkv_tok = []

        def copy_out(c0, n):
            def fin(t, bank, tok):
                r = act(partial(nc.scalar.activation, QKV[:, t, c0:c0 + n], bank, ACT.Copy), tok)
                qkv_tok.append(r)
                return r
            return fin

        rows_group(G["b1_q"], XT, xt, 512, copy_out(0, 512))
        rows_group(G["b1_kv"], XT, xt, 512, copy_out(512, 512))
        rows_group(G["b1_w"], XT, xt, 280, copy_out(1024, 280))

        places = [0, 1, 2, 3]
        sp_free, pt_free = [None] * 4, [None] * 4

        def head_scores(qT, kT, *tokens):
            bank, rel = take("aux")
            mm(PB[bank][:, 0:128], qT[:, 0:128], kT[:, 0:128], True, False, rel, *tokens)
            return bank, mm(PB[bank][:, 128:384], qT[:, 128:256], kT[:, 0:256], False, True, done=True)

        def head_softmax(bank, tok, bias, pre, post, gate, *tokens):
            i = places.pop(0)
            s = SP_[i]
            a = dve(partial(nc.vector.scalar_tensor_tensor, out=s, in0=PB[bank][:, 0:384], scalar=pre, in1=bias,
                                                     op0=ALU.mult, op1=ALU.add), tok, sp_free[i], *tokens)
            give("aux", bank, a)
            m, nm, sm, ri, gi = stat(2), stat(2), stat(2), stat(2), stat(2)
            dve(partial(nc.vector.tensor_reduce, m[:, 0:1], s[:, 0:128], AX.X, ALU.max), a)
            b = dve(partial(nc.vector.tensor_reduce, m[:, 1:2], s[:, 128:384], AX.X, ALU.max), a)
            c = dve(partial(nc.vector.tensor_scalar, nm, m, -post, None, ALU.mult), b)
            act(partial(nc.scalar.activation, s[:, 0:128], s[:, 0:128], ACT.Exp, bias=nm[:, 0:1], scale=post,
                                       accum_out=sm[:, 0:1]), c)
            d = act(partial(nc.scalar.activation, s[:, 128:384], s[:, 128:384], ACT.Exp, bias=nm[:, 1:2], scale=post,
                                           accum_out=sm[:, 1:2]), c)
            yield d
            f = dve(partial(nc.vector.reciprocal, ri, sm), d)
            if gate is not None:
                f = dve(partial(nc.vector.tensor_tensor, gi, ri, gate, ALU.mult), f)
                ri = gi
            act(partial(nc.scalar.activation, s[:, 0:128], s[:, 0:128], ACT.Copy, scale=ri[:, 0:1]), f)
            g = act(partial(nc.scalar.activation, s[:, 128:384], s[:, 128:384], ACT.Copy, scale=ri[:, 1:2]), f)
            return i, g

        def head_PT(i, tok):
            s = SP_[i]
            bank, rel = take("aux")
            o = PB[bank]
            for j in range(3):
                t = pe(partial(nc.tensor.transpose, o[:, j * P:j * P + P], s[:, j * P:j * P + P], ident), tok, rel,
                       done=(j == 2))
            sp_free[i] = t
            c = act(partial(nc.scalar.activation, PT[i], o[:, 0:384], ACT.Copy), t, pt_free[i])
            give("aux", bank, c)
            return c

        def bank_halves(p, b, *tokens):
            hh = act(partial(nc.scalar.activation, OT[:, p * 512:p * 512 + 256], PB[b][:, 0:256], ACT.Copy), *tokens)
            ll = dve(partial(nc.vector.tensor_tensor, OT[:, p * 512 + 256:p * 512 + 512], PB[b][:, 0:256],
                                               OT[:, p * 512:p * 512 + 256].bitcast(F32), ALU.subtract), hh)
            give("aux", b, ll)
            return [hh, ll]

        def in_flight(n, start, finished, most=3):
            active, nxt = [], 0
            while nxt < n or active:
                if nxt < n and len(active) < most and len(free["aux"]) >= 2:
                    gen = start(nxt)
                    active.append([nxt, gen, next(gen)])
                    nxt += 1
                for it in sorted(active, key=lambda it: when(it[2])):
                    it[2] = next(it[1], StopIteration)
                    if it[2] is StopIteration:
                        active.remove(it)
                        finished(it[0])
                        break
                    if it[2] is not None:
                        break
                todo = [it[2] for it in active if it[2] is not None]
                yield min(todo, key=when) if todo else (None if active else [])

        def b1_side():
            sq = SQ
            SS, RS, GG, GE = keep(24), keep(24), keep(48), keep(48)
            ssv = SS.rearrange("p (t h) -> p t h", t=2)
            rsv = RS.rearrange("p (t h) -> p t h", t=2)
            parts = ((0, 8, 0), (768, 2, 8), (1024, 2, 10))
            for c0, nh, h0 in parts:
                s = QKV[:, :, c0:c0 + 64 * nh]
                q = sq[:, 0:128 * nh]
                a = act(partial(nc.scalar.activation, q.rearrange("p (t n) -> p t n", t=2), s, ACT.Square),
                        qkv_tok, early, dve.last())
                r = dve(partial(nc.vector.tensor_reduce, 
                    ssv[:, :, h0:h0 + nh], q.rearrange("p (t h d) -> p t h d", t=2, d=64), AX.X, ALU.add), a)
            rr = rsqrt(RS, SS, 1.0 / 64, r)
            ge = act(partial(nc.scalar.activation, GE.rearrange("p (t n) -> p t n", t=2), QKV[:, :, 1280:1304], ACT.Exp,
                                            scale=-1.0), qkv_tok)
            g1 = dve(partial(nc.vector.tensor_scalar, GE, GE, 1.0, None, ALU.add), ge)
            g_tok = dve(partial(nc.vector.reciprocal, GG, GE), g1)
            ggv = GG.rearrange("p (t b h) -> p t b h", t=2, b=3)
            yield [rr, g_tok]
            nt = []
            for c0, nh, h0 in parts:
                for t in range(2):
                    s = QKV[:, t, c0:c0 + 64 * nh].rearrange("p (h d) -> p h d", d=64)
                    r = rsv[:, t, h0:h0 + nh].unsqueeze(2).broadcast_to([P, nh, 64])
                    nt.append(dve(partial(nc.vector.tensor_tensor, s, s, r, ALU.mult), rr))
            yield nt[-1]
            tt_tok = {}
            jobs = [(12, 512, None), (14, 640, None)] + [(2 * i, 128 * i, ("qg", 0)) for i in range(4)] + \
                   [(8, 768, ("kg", 1)), (10, 1024, ("kg", 2))]
            for n, (h0, c0, gain) in enumerate(jobs):
                while not free["aux"]:
                    yield
                bank, rel = take("aux")
                for j in range(2):
                    for t in range(2):
                        o = PB[bank][0:64, j * 256 + t * P:j * 256 + t * P + P]
                        s = QKV[:, t, c0 + 64 * j:c0 + 64 * j + 64]
                        tk = pe(partial(nc.tensor.transpose, o, s, ident), nt[-1], qkv_tok, rel,
                                done=(j == 1 and t == 1))
                d = TT[0:64, h0:h0 + 2, :].rearrange("p h n -> p (h n)")
                b = PB[bank][0:64, :]
                if gain is None:
                    c = act(partial(nc.scalar.activation, d, b, ACT.Copy), tk)
                else:
                    g = prm(gain[0], gain[1], 1, 64)
                    c = act(partial(nc.scalar.activation, d, b, ACT.Copy, scale=g), tk)
                give("aux", bank, c)
                tt_tok[h0] = tt_tok[h0 + 1] = c
                if n % 2:
                    yield
            while not free["aux"]:
                yield
            bank, rel = take("aux")
            kpf = None
            wtok = wc_tok
            for which, (h0, pos) in enumerate(((12, "posk"), (14, "posv"))):
                for g in range(2):
                    for half in range(2):
                        s = TT[0:64, h0 + g, 16 * half:16 * half + 240].rearrange("p (c j) -> p c j", j=16)
                        d = KP[:, 15 * g:15 * g + 15, 16 * half:16 * half + 16]
                        pp = prm(pos, 16 * half, 16, 64).unsqueeze(1).broadcast_to([64, 15, 16])
                        kt = dve(partial(nc.vector.tensor_tensor, d, s, pp, ALU.add), tt_tok[h0], kpf)
                yield [kt, wtok]
                for j in range(32):
                    kpf = mm(PB[bank][0:30, 64 * which:64 * which + 64], KP[:, :, j], WC[:, j, :], j == 0, j == 31,
                             kt, wtok, rel, done=(j == 31))
                if which == 0:
                    wtok = dma(WC, A["wcmp"][:, 2048:4096].rearrange("p (j e) -> p j e", j=32), kpf)
                yield kpf
            kc = keep(128)[0:30, :]
            c = act(partial(nc.scalar.activation, kc, PB[bank][0:30, 0:128], ACT.Copy), kpf)
            give("aux", bank, c)
            ks2, kss, krs = keep(64)[0:30, :], stat(1)[0:30, :], stat(1)[0:30, :]
            a = act(partial(nc.scalar.activation, ks2, kc[:, 0:64], ACT.Square, accum_out=kss), c)
            r = rsqrt(krs, kss, 1.0 / 64, a)
            kn = dve(partial(nc.vector.tensor_scalar, ks2, kc[:, 0:64], krs, None, ALU.mult), r)
            yield kn
            bank, rel = take("aux")
            t = pe(partial(nc.tensor.transpose, PB[bank][0:64, 0:30], ks2, ident[0:30, 0:30]), kn, rel)
            kcn = keep(30)[0:64, :]
            kcn_t = act(partial(nc.scalar.activation, kcn, PB[bank][0:64, 0:30], ACT.Copy, scale=prm("kg", 0, 1, 64)), t)
            give("aux", bank, kcn_t)
            yield kcn_t
            pcs = []
            for t in range(2):
                bank, rel = take("aux")
                for h in range(8):
                    m = mm(PB[bank][:, 30 * h:30 * h + 30], TT[0:64, h, t * P:t * P + P], kcn, h == 0, h == 7,
                           rel, kcn_t, tt_tok[h], done=(h == 7))
                pc = PC[:, t, :]
                pcv = pc.rearrange("p (h n) -> p h n", h=8)
                mx, sm, ri, gi = stat(8), stat(8), stat(8), stat(8)
                a = dve(partial(nc.vector.scalar_tensor_tensor, 
                    out=pc, in0=PB[bank][:, 0:240], scalar=0.125, in1=cbias[:, t, :], op0=ALU.mult, op1=ALU.add),
                    m, c2_tok)
                give("aux", bank, a)
                b = dve(partial(nc.vector.tensor_reduce, mx, pcv, AX.X, ALU.max), a)
                c = dve(partial(nc.vector.tensor_tensor, pcv, pcv, mx.unsqueeze(2).broadcast_to([P, 8, 30]),
                                                                  ALU.subtract), b)
                x = act(partial(nc.scalar.activation, pc, pc, ACT.Exp), c)
                f = dve(partial(nc.vector.tensor_tensor, pc, pc, cmask[:, t, :], ALU.mult), x)
                f = dve(partial(nc.vector.tensor_reduce, sm, pcv, AX.X, ALU.add), f)
                f = dve(partial(nc.vector.tensor_scalar, sm, sm, 1e-30, None, ALU.max), f)
                f = dve(partial(nc.vector.reciprocal, ri, sm), f)
                f = dve(partial(nc.vector.tensor_tensor, gi, ri, ggv[:, t, 0, :], ALU.mult), f, g_tok)
                pcs.append(dve(partial(nc.vector.tensor_tensor, 
                    pcv, pcv, gi.unsqueeze(2).broadcast_to([P, 8, 30]), ALU.mult), f))
                yield pcs[-1]
            ptc = {}
            for p in range(4):
                while not free["aux"]:
                    yield
                bank, rel = take("aux")
                for j in range(2):
                    for t in range(2):
                        o = PB[bank][0:30, j * 256 + t * P:j * 256 + t * P + P]
                        s = PC[:, t, 30 * (2 * p + j):30 * (2 * p + j) + 30]
                        tk = pe(partial(nc.tensor.transpose, o, s, ident), pcs[1], rel, done=(j == 1 and t == 1))
                ptc[p] = act(partial(nc.scalar.activation, 
                    PTC[:, 2 * p:2 * p + 2, :].rearrange("p h n -> p (h n)"), PB[bank][0:30, :], ACT.Copy), tk, kpf)
                give("aux", bank, ptc[p])
            yield ptc[3]

            def item(h, branch, acc):
                g = h // 4
                koff = (8, 10)[branch]
                voff = (896, 1152)[branch]
                while not free["aux"]:
                    yield
                bank, tk = head_scores(TT[0:64, h, :], TT[0:64, koff + g, :], tt_tok[h], tt_tok[koff])
                slope = 2.0 ** -(h + 1)
                yield tk
                i, tk = yield from head_softmax(bank, tk, distb, 0.125 / slope, slope, ggv[:, :, 1 + branch, h], g_tok)
                yield tk
                while not free["aux"]:
                    yield
                c = head_PT(i, tk)
                yield c
                o = PB[acc[0]]
                r0 = 64 * (h % 2)
                if branch == 0:
                    mm(o[r0:r0 + 64, 0:256], kc[:, 64:128], PTC[:, h, :], True, False, acc[1], ptc[h // 2])
                mm(o[r0:r0 + 64, 0:256], QKV[:, 0, voff + 64 * g:voff + 64 * g + 64], PT[i][:, 0:256], False, False, c)
                pt_free[i] = mm(o[r0:r0 + 64, 128:256], QKV[:, 1, voff + 64 * g:voff + 64 * g + 64],
                                PT[i][:, 256:384], False, branch == 1, done=True)
                places.append(i)
                done_items[h] = pt_free[i]

            done_items = {}
            accs = {}
            n_done = {}

            def start(j):
                h, b = j // 2, j % 2
                if h // 2 not in accs:
                    accs[h // 2] = take("aux")
                return item(h, b, accs[h // 2])

            def finished(j):
                p = j // 4
                n_done[p] = n_done.get(p, 0) + 1
                if n_done[p] == 4:
                    b = accs[p][0]
                    o_tok[p] = bank_halves(p, b, done_items[2 * p], done_items[2 * p + 1])

            yield from in_flight(16, start, finished, 4)

        o_tok = {}
        add_side(b1_side())

        z_tok = {}
        u0 = dve(partial(nc.vector.memset, UU[:, :, 0:2], 0.0))
        cc_tok, uu_free, uu_tok = {}, [None] * 4, {}

        def fin_c(i):
            def fin(f, L, R, tok):
                cc_tok[f] = join(CC[:, f, :], L, R, tok)
                return cc_tok[f]
            return fin

        def fin_x(i):
            def fin(f, L, R, tok):
                u, v = UU[:, f, :], CC[:, f, :]
                r = join(u[:, 2:258], L, R, tok, u0, z_tok.get(4 * (i - 1) + f))

                def taps():
                    ft = 4 * i + f
                    d = dve(partial(nc.vector.tensor_tensor, u[:, 2:258], u[:, 2:258], v, ALU.mult), r, cc_tok[f])
                    d = dve(partial(nc.vector.tensor_scalar, v, u[:, 0:256], prm("convw", ft), None, ALU.mult), d)
                    for k in (1, 2):
                        d = dve(partial(nc.vector.scalar_tensor_tensor, out=v, in0=u[:, k:k + 256],
                                        scalar=prm("convw", 8 * k + ft), in1=v, op0=ALU.mult, op1=ALU.add), d)
                    uu_tok[f] = d
                spread.append(taps)
                return r
            return fin

        def fin_b(i):
            def fin(f, L, R, tok):
                while spread:
                    spread.pop(0)()
                y = UU[:, f, 2:258]
                j = join(y, L, R, tok, uu_tok[f])

                def split_z():
                    ft = 4 * i + f
                    z = dve(partial(nc.vector.tensor_tensor, y, y, CC[:, f, :], ALU.mult), j)
                    z_tok[ft] = halves(ZT[:, ft * 512:ft * 512 + 512], y, z)
                spread.append(split_z)
                return j
            return fin

        for i in range(2):
            cols_group(G[f"b1_c{i}"], XT, xt, fin_c(i))
            cols_group(G[f"b1_x{i}"], XT, xt, fin_x(i))
            cols_group(G[f"b1_b{i}"], XT, xt, fin_b(i))
        while spread:
            spread.pop(0)()
        after_conv = fence()

        GA = W[:, 12784:14832].rearrange("p (t n) -> p t n", t=2)
        GB = W[:, 16240:18288].rearrange("p (t n) -> p t n", t=2)
        g_toks = {}

        def fin_gate(G_, i, key):
            def fin(t, bank, tok):
                r = act(partial(nc.scalar.activation, G_[:, t, 512 * i:512 * i + 512], bank, ACT.Copy), tok, after_conv)
                g_toks[key, i, t] = r
                return r
            return fin

        def sigmoid(G_, toks_):
            return [act(partial(nc.scalar.activation, G_[:, t, :], G_[:, t, :], ACT.Sigmoid), toks_(t))
                    for t in range(2)]

        for i in range(2):
            rows_group(G[f"b1_gb{i}"], XT, xt, 512, fin_gate(GB, i, "b"))
        for i in range(2):
            rows_group(G[f"b1_ga{i}"], XT, xt, 512, fin_gate(GA, i, "a"))
        xn_free = pe.last()
        gb_tok = sigmoid(GB, lambda t: [g_toks["b", 0, t], g_toks["b", 1, t]])
        ga_tok = sigmoid(GA, lambda t: [g_toks["a", 0, t], g_toks["a", 1, t]])
        b_tok, a_tok = {}, {}

        def fin_times(G_, gate_tok, toks_, i, other=None):
            def fin(t, bank, tok):
                g = G_[:, t, 512 * i:512 * i + 512]
                r = toks_[i, t] = dve(partial(nc.vector.tensor_tensor, g, bank, g, ALU.mult), tok, gate_tok[t])
                if other is not None:
                    o, o_toks = other
                    toks_[i, t] = dve(partial(nc.vector.tensor_tensor, g, g, o[:, t, 512 * i:512 * i + 512], ALU.add),
                                      r, o_toks[i, t])
                return r
            return fin

        for i in range(2):
            rows_group(G[f"b1_wb{i}"], ZT, z_tok, 512, fin_times(GB, gb_tok, b_tok, i))
        flush()
        after_attn = fence()
        places.remove(3)
        for i in range(2):
            rows_group(G[f"b1_wa{i}"], OT, o_tok, 512, fin_times(GA, ga_tok, a_tok, i, (GB, b_tok)))
        ot_free = pe.last()
        mt = {}
        drain(to_T(mt, W[:, 12784:14832], [[a_tok[0, t], a_tok[1, t]] for t in range(2)], XT, None, xn_free))

        x_cur = {}

        def fin_add(i, *tokens):
            def fin(t, bank, tok):
                m = X[:, t * D + 512 * i:t * D + 512 * i + 512]
                r = dve(partial(nc.vector.tensor_tensor, m, m, bank, ALU.add), tok, *tokens)
                x_cur[i, t] = r
                return r
            return fin

        def x_toks():
            return [[x_cur[0, t], x_cur[1, t]] for t in range(2)]

        SQB = W[:, 8192:9216]
        MEM = W[:, 10480:12528]
        memv = A["mem_2"].rearrange("o (t p) d -> p (o t) d", p=P)
        mem_tok = [dma(MEM[:, 0:D], memv[:, 0, :], after_attn), dma(MEM[:, D:2 * D], memv[:, 1, :], after_attn)]
        memT = {}

        def mem_side():
            mn = norm_rows(MEM, MEM, SQB, [[m, m] for m in mem_tok], after_attn)
            yield mn[1]
            yield from to_T(memT, MEM, mn, OT, "normmem", ot_free)

        add_side(mem_side())
        for i in range(2):
            rows_group(G[f"b1_wo{i}"], XT, mt, 512, fin_add(i))
        flush()

        HF = W[:, 9216:9728].rearrange("p (i n) -> p i n", i=2)
        XS = W[:, 4096:6144]
        hf_free = [None, None]

        def ffn(tag, xt_toks):
            assert len(free["aux"]) == 4
            accs = [take("aux") for _ in range(4)]
            ht_free = [None, None]
            ht = {}
            k_n = [0]

            def up(c):
                def fin(f, L, R, tok):
                    i = (4 * c + f) % 2
                    j = join(HF[:, i, :], L, R, tok, hf_free[i])
                    v = dve(partial(nc.vector.scalar_tensor_tensor, out=HF[:, i, :], in0=HF[:, i, :], scalar=0.0,
                                                             in1=HF[:, i, :], op0=ALU.max, op1=ALU.mult), j)
                    a = (4 * (c % 2) + f) * 512
                    h = act(partial(nc.scalar.activation, ZT[:, a:a + 256], HF[:, i, :], ACT.Copy), v, ht_free[c % 2])
                    l = dve(partial(nc.vector.tensor_tensor, ZT[:, a + 256:a + 512], HF[:, i, :],
                                                      ZT[:, a:a + 256].bitcast(F32), ALU.subtract), h)
                    hf_free[i] = l
                    ht[c, f] = [h, l]
                    return j
                cols_group(G[f"{tag}_up{c}"], XT, xt_toks, fin)

            def down(c):
                for i in range(2):
                    for n, u in enumerate(G[f"{tag}_dn{c}_{i}"]):
                        def fn(h, l, tokens):
                            for k in range(2):
                                kt = 2 * n + k
                                for t in range(2):
                                    b, rel = accs[2 * i + t]
                                    o = PB[b][:, :]
                                    a = (4 * (c % 2) + kt) * 512
                                    xh = ZT[:, a + t * P:a + t * P + P]
                                    xl = ZT[:, a + 256 + t * P:a + 256 + t * P + P]
                                    mm(o, xh, h[:, k, :], c == 0 and kt == 0, False, tokens, ht[c, kt], rel)
                                    mm(o, xh, l[:, k, :], False, False)
                                    last = mm(o, xl, h[:, k, :], False, c == 7 and kt == 3, done=(k == 1))
                                    if k == 1:
                                        fin_tok[i, t] = last
                            return last
                        use(u, fn)
                ht_free[c % 2] = pe.last()

            fin_tok = {}
            for c in range(8):
                up(c)
                if c:
                    down(c - 1)
            down(7)
            for i in range(2):
                for t in range(2):
                    b, _ = accs[2 * i + t]
                    r = fin_add(i)(t, PB[b][:, :], fin_tok[i, t])
                    give("aux", b, r)

        def norm_to_XT(into, gain):
            w_free = pe.last()
            n = norm_rows(X, XS, SQB, x_toks(), w_free)
            yield [n[0], n[1]]
            yield from to_T(into, XS, n, XT, gain, w_free)

        KXT = KV[:, 0:1024].rearrange("p (h n) -> p h n", h=4)
        VX = KV[:, 1024:2048].rearrange("p (t n) -> p t n", t=2)
        kx_tok, vx_tok = {}, {}

        def fin_kx(f, L, R, tok):
            kx_tok[f] = join(KXT[:, f, :], L, R, tok)
            return kx_tok[f]

        def fin_vx(t, bank, tok):
            vx_tok[t] = act(partial(nc.scalar.activation, VX[:, t, :], bank, ACT.Copy), tok)
            return vx_tok[t]

        ht = {}
        add_side(norm_to_XT(ht, "norm2"))
        cols_group(G["mk"], OT, memT, fin_kx)
        flush()
        ffn("f1", ht)

        xt = {}
        add_side(norm_to_XT(xt, "normmix"))
        rows_group(G["mv"], OT, memT, 512, fin_vx)
        flush()
        start2 = fence()

        QT2 = W[:, 0:2048].rearrange("p (h n) -> p h n", h=8)
        KT2 = W[:, 2048:4096].rearrange("p (h n) -> p h n", h=8)
        V2 = W[:, 4096:6144].rearrange("p (t n) -> p t n", t=2)
        U2 = W[:, 6144:8432].rearrange("p (f n) -> p f n", f=8)
        YC = W[:, 8432:10480].rearrange("p (f n) -> p f n", f=8)
        QI = W[:, 12784:13808].rearrange("p (f n) -> p f n", f=4)
        KI = W[:, 13808:14064]
        SG = W[:, 14064:14576].rearrange("p (i n) -> p i n", i=2)
        SC = W[:, 14832:15216]
        BG = W[:, 15728:16240]
        WI = ST[:, 496:512]
        qi_tok, q2_tok, k2_tok, v2_tok = {}, {}, {}, {}

        def fin_cols(dst, toks_, i, *tokens):
            def fin(f, L, R, tok):
                toks_[4 * i + f] = join(dst[:, 4 * i + f, :], L, R, tok, *tokens)
                return toks_[4 * i + f]
            return fin

        sel_tok, sel_free = {}, {}

        def index_side():
            acc = None
            for h in range(8):
                while not free["aux"]:
                    yield
                r0 = 64 * (h % 2)
                bank, tk = head_scores(QI[r0:r0 + 64, h // 2, :], KI[r0:r0 + 64, :], qi_tok[h // 2], ki_tok["k"])
                i = places.pop(0)
                r = SP_[i]
                a = act(partial(nc.scalar.activation, r, PB[bank][:, 0:384], ACT.Relu, scale=0.125),
                        tk, sp_free[i])
                give("aux", bank, a)
                base = causal if h == 0 else SC
                for t, (c0, c1) in enumerate(((0, 128), (128, 384))):
                    acc = dve(partial(nc.vector.scalar_tensor_tensor, 
                        out=SC[:, c0:c1], in0=r[:, c0:c1], scalar=WI[:, 8 * t + h:8 * t + h + 1],
                        in1=base[:, c0:c1], op0=ALU.mult, op1=ALU.add), a, ki_tok["w"], acc, start2)
                sp_free[i] = acc
                places.append(i)
                yield acc
            last = {0: acc, 1: acc}
            for rnd in range(8):
                ms = []
                for t, (c0, c1) in enumerate(((0, 128), (128, 384))):
                    m8 = stat(8)
                    ms.append((m8, dve(partial(nc.vector.max, m8, SC[:, c0:c1]), last[t])))
                for t, (c0, c1) in enumerate(((0, 128), (128, 384))):
                    m8, tk = ms[t]
                    last[t] = dve(partial(nc.vector.match_replace, 
                        out=SC[:, c0:c1], in_to_replace=m8, in_values=SC[:, c0:c1], imm_value=-3e38), tk)
                yield last[1]
            a = dve(partial(nc.vector.tensor_scalar, SC, SC, -2e38, NEG, ALU.is_gt, ALU.mult), last[0], last[1])
            sel_tok[0] = dve(partial(nc.vector.tensor_tensor, SC, SC, causal, ALU.add), a)


        sg_free = [None, None]
        sg_tok = {}
        u2z = dve(partial(nc.vector.memset, U2[:, :, 0:30], 0.0), start2)
        u2_tok = {}

        def fin_cg(i):
            def fin(f, L, R, tok):
                d = join(GS[:, f, :], L, R, tok, gs_free.get(f), start2)

                def sig():
                    sg_tok[f] = act(partial(nc.scalar.activation, GS[:, f, :], GS[:, f, :], ACT.Sigmoid), d)
                later.append(sig)
                return d
            return fin

        GS = W[:, 4096:5120].rearrange("p (f n) -> p f n", f=4)
        gs_free = {}

        def fin_ca(i):
            def fin(f, L, R, tok):
                u_ = U2[:, 4 * i + f, 30:286]
                d = join(u_, L, R, tok, start2)

                def gate():
                    u2_tok[4 * i + f] = gs_free[f] = dve(
                        partial(nc.vector.tensor_tensor, u_, u_, GS[:, f, :], ALU.mult), d, sg_tok[f])
                later.append(gate)
                return d
            return fin

        zc_tok = {}
        conv_done = [False]

        y = {}

        def conv_pe_side():
            dg_free = [None] * 4
            for f in range(PE_CONV, 8):
                while f not in u2_tok:
                    yield
                while len(free["aux"]) < 2:
                    yield
                bank, rel = take("aux")
                for k in range(31):
                    i = k % 4
                    d = DG[:, P * i:P * i + P]
                    t = act(partial(nc.scalar.activation, d, ident, ACT.Copy, scale=prm("convw2", 8 * k + f)), dg_free[i])
                    dg_free[i] = mm(PB[bank][:, 0:256], d, U2[:, f, k:k + 256], k == 0, k == 30, t, rel,
                                    u2_tok[f], u2z, done=True)
                    yield []
                r = dve(partial(nc.vector.tensor_scalar, YC[:, f, :], PB[bank][:, 0:256], prm("convb2", f), None,
                                ALU.add), dg_free[i], start2)
                give("aux", bank, r)
                y[f] = r

        def conv_side():
            for f0 in range(0, PE_CONV, 2):
                while f0 + 1 not in u2_tok:
                    yield
                fs = (f0, f0 + 1)
                for f in fs:
                    y[f] = dve(partial(nc.vector.tensor_scalar, YC[:, f, :], U2[:, f, 0:256], prm("convw2", f),
                                       prm("convb2", f), ALU.mult, ALU.add), u2_tok[f], u2z, start2)
                for k in range(1, 31):
                    for f in fs:
                        y[f] = dve(partial(nc.vector.scalar_tensor_tensor, out=YC[:, f, :], in0=U2[:, f, k:k + 256],
                                           scalar=prm("convw2", 8 * k + f), in1=YC[:, f, :], op0=ALU.mult,
                                           op1=ALU.add), y[f])
                    yield []
            while len(y) < 8:
                yield
            conv_done[0] = fence()
            yall = W[:, 8432:10480]
            while not free["aux"]:
                yield
            bank, rel = take("aux")
            for f in range(8):
                tk = mm(PB[bank][:, 0:256], ones, YC[:, f, :], f == 0, f == 7, y[f], rel, done=(f == 7))
            mu = U2[:, 0, 0:256]
            m = act(partial(nc.scalar.activation, mu, PB[bank][:, 0:256], ACT.Copy, scale=1.0 / D), tk, conv_done[0])
            give("aux", bank, m)
            yield m
            c = dve(partial(nc.vector.tensor_tensor, YC, YC, mu.unsqueeze(1).broadcast_to([P, 8, 256]), ALU.subtract), m)
            sqs = W[:, 6144 + 286:6144 + 286 + 512].rearrange("p (i n) -> p i n", i=2)
            yield c
            while not free["aux"]:
                yield
            bank, rel = take("aux")
            fr = [None, None]
            for f in range(8):
                q = sqs[:, f % 2, :]
                a = act(partial(nc.scalar.activation, q, YC[:, f, :], ACT.Square), c, fr[f % 2])
                fr[f % 2] = tk = mm(PB[bank][:, 0:256], ones, q, f == 0, f == 7, a, rel, done=True)
                yield a
            v, r = U2[:, 4, 0:256], U2[:, 5, 0:256]
            a = dve(partial(nc.vector.tensor_scalar, v, PB[bank][:, 0:256], 1.0 / D, EPS, ALU.mult, ALU.add), tk)
            give("aux", bank, a)
            while len(o2_tok) < 8:
                yield
            b = act(partial(nc.scalar.activation, v, v, ACT.Sqrt), a)
            r_t = dve(partial(nc.vector.reciprocal, r, v), b)
            c = dve(partial(nc.vector.tensor_tensor, YC, YC, r.unsqueeze(1).broadcast_to([P, 8, 256]), ALU.mult), r_t)
            yield
            for f in range(8):
                s = act(partial(nc.scalar.activation, YC[:, f, :], YC[:, f, :], ACT.Silu, scale=prm("lng", f),
                                bias=prm("lnb", f)), c)
                zc_tok[f] = halves(ZT[:, f * 512:f * 512 + 512], YC[:, f, :], s, start2)
                yield []
            conv_done.append(fence())

        def conv_groups(i):
            cols_group(G[f"b2_cg{i}"], XT, xt, fin_cg(i))
            cols_group(G[f"b2_ca{i}"], XT, xt, fin_ca(i))

        conv_groups(0)
        add_side(conv_side(), first=False)
        add_side(conv_pe_side(), first=False, uses=(act,))
        cols_group(G["b2_qi"], XT, xt, fin_cols(QI, qi_tok, 0, start2))

        bk, rk = take("main")
        bw, rw = take("main")
        ki_tok = {}

        def fn_ki(h, l, tokens):
            for k in range(8):
                a = k * 512
                mm(PB[bk][:, :], h[:, k, :], XT[:, a:a + 512], k == 0, False, tokens, xt[k], rk)
                last = mm(PB[bk][:, 0:256], l[:, k, :], XT[:, a:a + 256], False, k == 7, done=(k == 7))
            ki_tok["k"] = join(KI, PB[bk][:, 0:256], PB[bk][:, 256:512], last, start2)
            give("main", bk, ki_tok["k"])
            return last

        def fn_wi(h, l, tokens):
            for t in range(2):
                for k in range(8):
                    a = k * 512 + t * P
                    o = PB[bw][:, 8 * t:8 * t + 8]
                    mm(o, XT[:, a:a + P], h[:, k, :], k == 0 and t == 0, False, tokens, rw)
                    mm(o, XT[:, a:a + P], l[:, k, :], False, False)
                    last = mm(o, XT[:, a + 256:a + 256 + P], h[:, k, :], False, k == 7 and t == 1,
                              done=(k == 7 and t == 1))
            ki_tok["w"] = act(partial(nc.scalar.activation, WI, PB[bw][:, 0:16], ACT.Copy, scale=8.0 ** -0.5), last)
            give("main", bw, ki_tok["w"])
            return last

        use(G["b2_ki"][0], fn_ki)
        use(G["b2_ki"][1], fn_wi)

        add_side(index_side())
        conv_groups(1)
        gs_end = fence()
        for i in range(2):
            cols_group(G[f"b2_k{i}"], XT, xt, fin_cols(KT2, k2_tok, i, start2))
        for i in range(2):
            cols_group(G[f"b2_q{i}"], XT, xt, fin_cols(QT2, q2_tok, i, start2))

        def fin_v(i):
            def fin(t, bank, tok):
                v2_tok[i, t] = act(partial(nc.scalar.activation, V2[:, t, 512 * i:512 * i + 512], bank, ACT.Copy), tok, gs_end)
                return v2_tok[i, t]
            return fin

        for i in range(2):
            rows_group(G[f"b2_v{i}"], XT, xt, 512, fin_v(i))

        o2_tok = {}

        def dsa_side():
            while 0 not in sel_tok:
                yield

            def item(h):
                while not free["aux"]:
                    yield
                bank, tk = head_scores(QT2[:, h, :], KT2[:, h, :], q2_tok[h], k2_tok[h])
                yield tk
                i, tk = yield from head_softmax(bank, tk, SC, 128.0 ** -0.5, 1.0, None, sel_tok[0])
                yield tk
                while not free["aux"]:
                    yield
                c = head_PT(i, tk)
                yield c
                while not free["aux"]:
                    yield
                bank, rel = take("aux")
                o = PB[bank]
                mm(o[:, 0:256], V2[:, 0, h * P:h * P + P], PT[i][:, 0:256], True, False, c, rel, v2_tok[h // 4, 0])
                pt_free[i] = mm(o[:, 128:256], V2[:, 1, h * P:h * P + P], PT[i][:, 256:384], False, True,
                                v2_tok[h // 4, 1], done=True)
                places.append(i)
                yield pt_free[i]
                o2_tok[h] = bank_halves(h, bank, pt_free[i])

            yield from in_flight(8, item, lambda h: None)

        add_side(dsa_side())

        GA2 = W[:, 12784:14832].rearrange("p (t n) -> p t n", t=2)
        GC2 = W[:, 16240:18288].rearrange("p (t n) -> p t n", t=2)
        raw_tok = {}
        bg_free = [None]

        def gate_group(name, i, dst, off, *tokens):
            bt = dma(BG, A["b_gate_2"][:, off + 512 * i:off + 512 * i + 512].broadcast_to([P, 512]), bg_free[0], start2)

            def fin(t, bank, tok):
                r = dve(partial(nc.vector.tensor_tensor, dst[:, t, 512 * i:512 * i + 512], bank, BG, ALU.add), tok, bt, *tokens)
                raw_tok[name, i, t] = bg_free[0] = r
                return r
            rows_group(G[f"b2_{name}{i}"], XT, xt, 512, fin)

        for i in range(2):
            gate_group("gc", i, GC2, 0)
        while 0 not in sel_tok:
            turn()
        idx_end = fence()
        for i in range(2):
            gate_group("ga", i, GA2, 1024, idx_end)
        while len(o2_tok) < 8:
            turn()
        ga_tok = sigmoid(GA2, lambda t: [raw_tok["ga", 0, t], raw_tok["ga", 1, t]])
        gc_tok = sigmoid(GC2, lambda t: [raw_tok["gc", 0, t], raw_tok["gc", 1, t]])
        a_tok, c_tok = {}, {}
        for i in range(2):
            rows_group(G[f"b2_wa{i}"], OT, o2_tok, 512, fin_times(GA2, ga_tok, a_tok, i))
        flush()
        for i in range(2):
            rows_group(G[f"b2_wc{i}"], ZT, zc_tok, 512, fin_times(GC2, gc_tok, c_tok, i, (GA2, a_tok)))
        xfree = pe.last()
        mt = {}
        drain(to_T(mt, W[:, 16240:18288], [[c_tok[0, t], c_tok[1, t]] for t in range(2)], XT, None, xfree))
        for i in range(2):
            rows_group(G[f"b2_wm{i}"], XT, mt, 512, fin_add(i))

        xt = {}
        drain(norm_to_XT(xt, "normx"))
        QX = W[:, 0:1024].rearrange("p (h n) -> p h n", h=4)
        S5 = W[:, 1024:3072].rearrange("p (i n) -> p i n", i=4)
        P5 = W[:, 6144:8192].rearrange("p (i n) -> p i n", i=4)
        qx_tok, ox_tok = {}, {}
        cols_group(G["xq"], XT, xt, fin_cols(QX, qx_tok, 0, fence()))
        cross_places = [0, 1, 2, 3]
        s5_free, p5_free = [None] * 4, [None] * 4
        XSC = 128.0 ** -0.5

        def cross_item(h):
            while not free["aux"]:
                yield
            bank, rel = take("aux")
            o = PB[bank]
            for t in range(2):
                tk = mm(o[:, 256 * t:256 * t + 256], QX[:, h, t * P:t * P + P], KXT[:, h, :], t == 0, t == 1,
                        rel, qx_tok[h], kx_tok[h], done=(t == 1))
            i = cross_places.pop(0)
            s = S5[:, i, :]
            m, nm, sm, ri = stat(2), stat(2), stat(2), stat(2)
            a = dve(partial(nc.vector.tensor_reduce, m, o[:, :].rearrange("p (t n) -> p t n", t=2), AX.X, ALU.max), tk)
            b = dve(partial(nc.vector.tensor_scalar, nm, m, -XSC, None, ALU.mult), a)
            for t in range(2):
                c = act(partial(nc.scalar.activation, s[:, 256 * t:256 * t + 256], o[:, 256 * t:256 * t + 256], ACT.Exp,
                                                    bias=nm[:, t:t + 1], scale=XSC, accum_out=sm[:, t:t + 1]),
                        b, s5_free[i])
            give("aux", bank, c)
            yield
            f = dve(partial(nc.vector.reciprocal, ri, sm), c)
            for t in range(2):
                g = dve(partial(nc.vector.tensor_scalar, s[:, 256 * t:256 * t + 256], s[:, 256 * t:256 * t + 256],
                                                       ri[:, t:t + 1], None, ALU.mult), f)
            yield
            while not free["aux"]:
                yield
            bank2, rel = take("aux")
            o2 = PB[bank2]
            for k in range(2):
                for t in range(2):
                    tk = pe(partial(nc.tensor.transpose, o2[:, 256 * k + P * t:256 * k + P * t + P],
                                                            s[:, 256 * t + P * k:256 * t + P * k + P], ident),
                            g, rel, done=(k == 1 and t == 1))
            s5_free[i] = tk
            c = act(partial(nc.scalar.activation, P5[:, i, :], o2[:, :], ACT.Copy), tk, p5_free[i])
            give("aux", bank2, c)
            yield
            while not free["aux"]:
                yield
            bank3, rel = take("aux")
            o3 = PB[bank3]
            for k in range(2):
                tk = mm(o3[:, 0:256], VX[:, k, h * P:h * P + P], P5[:, i, 256 * k:256 * k + 256], k == 0, k == 1,
                        c, rel, vx_tok[k], done=(k == 1))
            p5_free[i] = tk
            cross_places.append(i)
            ox_tok[h] = bank_halves(h, bank3, tk)

        for _ in in_flight(4, cross_item, lambda h: None, 4):
            pass
        for i in range(2):
            rows_group(G[f"xo{i}"], OT, ox_tok, 512, fin_add(i))
        ht = {}
        drain(norm_to_XT(ht, "normffn"))
        GF = W[:, 0:1024]
        gf_tok = dma(GF, A["norm_final_g_2"].broadcast_to([P, D]), fence())
        ffn("f2", ht)

        n = norm_rows(X, XS, SQB, x_toks(), gf_tok, gain=GF)
        outv = out.rearrange("o (t p) d -> p (o t) d", p=P)
        s_out = sem("stored")
        for t in range(2):
            o = XS[:, t * D:t * D + D]
            sp.wait(n[t])
            sp.queue.append(partial(signalling, partial(nc.sync.dma_start, outv[:, t, :], o), s_out, 16))
        sp.wait((s_out, 32, 0))

        block = ctx.enter_context(nc.Block())

        @block.sync
        def _(e):
            for f in sp.queue:
                f()

        @block.tensor
        def _(e):
            for f in pe.queue:
                f()

        @block.scalar
        def _(e):
            for f in act.queue:
                f()

        @block.vector
        def _(e):
            for f in dve.queue:
                f()

        @block.gpsimd
        def _(e):
            for f in pool.queue:
                f()


def constants():
    c = np.zeros((P, CS["end"]), np.float32)
    c[:, 0:128] = np.eye(P)
    c[:, 128:256] = 1.0
    c[:, CS["mhalf"]] = -0.5
    q, k = np.arange(P)[:, None], np.arange(2 * P)[None, :]
    for c0, t, n in ((0, 0, 128), (128, 1, 256)):
        d = (q + P * t - k[:, :n]).astype(np.float32)
        c[:, CS["dist"] + c0:CS["dist"] + c0 + n] = np.where(d >= 0, -d, -1e33)
        c[:, CS["causal"] + c0:CS["causal"] + c0 + n] = np.where(d >= 0, 0, NEG)
    c2 = np.zeros((P, C2["end"]), np.float32)
    b = c2[:, 0:480].reshape(P, 2, 8, 2, 15)
    m = c2[:, 480:960].reshape(P, 2, 8, 2, 15)
    cend = 16 * np.arange(15) + 31
    b[:] = NEG
    for t in range(2):
        d = (np.arange(P)[:, None] + P * t - cend[None, :]).astype(np.float32)
        for h in range(8):
            slope = np.float32(2.0 ** -(h + 1))
            b[:, t, h, h // 4] = np.where(d >= 0, -slope * d, NEG)
            m[:, t, h, h // 4] = d >= 0
    return c, c2


def kernel(**inputs):
    import concourse.bacc as bacc
    from concourse.bass_utils import run_bass_kernel_spmd

    I = {k: np.asarray(v) for k, v in inputs.items()}
    params = np.zeros((P, NPRM), np.float32)

    def tiles(v):
        return v.reshape(-1, 8, P).transpose(2, 0, 1).reshape(P, -1)

    for name, key in (("norm1", "norm1_g"), ("norm2", "norm2_g"), ("convw", "conv_w"), ("normmix", "norm_mix_g_2"),
                      ("convw2", "conv_w_2"), ("convb2", "conv_b_2"), ("lng", "conv_ln_g_2"), ("lnb", "conv_ln_b_2"),
                      ("normx", "norm_x_g_2"), ("normmem", "norm_mem_g_2"), ("normffn", "norm_ffn_g_2")):
        v = tiles(I[key].reshape(-1, D))
        params[:, PRM[name]:PRM[name] + v.shape[1]] = v
    params[0:64, PRM["qg"]] = I["q_norm_g"][0]
    params[0:64, PRM["kg"]:PRM["kg"] + 3] = I["k_norm_g"][0].T
    params[0:64, PRM["posk"]:PRM["posk"] + 32] = I["cmp_pos_k"][0].T
    params[0:64, PRM["posv"]:PRM["posv"] + 32] = I["cmp_pos_v"][0].T
    wcmp = np.concatenate([I[k][0].reshape(32, 64, 64).transpose(1, 0, 2).reshape(64, 2048)
                           for k in ("w_cmp_k", "w_cmp_v")], axis=1)
    c, c2 = constants()
    arrays = {"params": params, "consts": c, "consts2": c2, "wcmp": wcmp, "x": I["x"], "mem_2": I["mem_2"],
              "b_gate_2": I["b_gate_2"], "norm_final_g_2": I["norm_final_g_2"].reshape(1, D)}
    for k in ("w_in", "w_branch_a", "w_branch_b", "w_out", "w_up", "w_down", "w_in_2", "w_conv_out_2",
              "w_attn_out_2", "w_mix_out_2", "wx_q_2", "wx_kv_2", "wx_o_2", "w_ff1_2", "w_ff2_2"):
        arrays[k] = I[k][0]
    nc = bacc.Bacc("TRN2", target_bir_lowering=False, num_devices=1)
    arrays = {k: np.ascontiguousarray(v) for k, v in arrays.items()}
    A = {k: nc.dram_tensor(f"in_{k}", v.shape, mybir.dt.from_np(v.dtype), kind="ExternalInput").ap()
         for k, v in arrays.items()}
    out = nc.dram_tensor("out_0", (1, 256, D), F32, kind="ExternalOutput").ap()
    build(nc, A, out)
    r = run_bass_kernel_spmd(nc, [{f"in_{k}": v for k, v in arrays.items()}], core_ids=[0])
    return r.results[0]["out_0"]
```
